# Optimizing a Trainium2 kernel written in Bass

```python
import jax, jax.numpy as jnp
from jax import lax
import numpy as np
import math

D_MODEL = 1024
BATCH = 1
SEQ = 512
DEPTH = 4

N_MIXERS = 3
EXPAND = 2
D_INNER = EXPAND * D_MODEL
POOL_WINDOWS = (2, 4, 8, 16)
N_POOL_GROUPS = len(POOL_WINDOWS)
POOL_GROUP = D_INNER // N_POOL_GROUPS
CONV_WIDTH = 3
N_HEADS = 16
QK_NOPE_DIM = 128
QK_ROPE_DIM = 64
V_HEAD_DIM = D_INNER // N_HEADS
Q_LORA_RANK = 384
KV_LORA_RANK = 256
MLA_IN_DIM = Q_LORA_RANK + KV_LORA_RANK + QK_ROPE_DIM + D_INNER
ATTN_SCALE = (QK_NOPE_DIM + QK_ROPE_DIM) ** -0.5
ROPE_BASE = 10000.0
Q_BLOCK = 128
NORM_EPS = 1e-6
MAX_POS_OFFSET = 1024
N_POOL = (DEPTH + 2) // 3
N_CONV = (DEPTH + 1) // 3
N_MLA = DEPTH // 3


def rms_norm(x, g):
    xf = x.astype(jnp.float32)
    y = xf * lax.rsqrt(jnp.mean(xf * xf, axis=-1, keepdims=True) + NORM_EPS)
    return (y * g.astype(jnp.float32)).astype(x.dtype)

def pool_mixer(xn, w_in, w_grp, scale, w_out):
    B, S, _ = xn.shape
    u, z = jnp.split(xn @ w_in, 2, axis=-1)
    uf = u.astype(jnp.float32).reshape(B, S, N_POOL_GROUPS, POOL_GROUP)
    cs = jnp.cumsum(uf, axis=1)
    count_base = jnp.arange(1, S + 1, dtype=jnp.float32)
    pooled = []
    for g, w in enumerate(POOL_WINDOWS):
        c = cs[:, :, g]
        prev = jnp.pad(c, ((0, 0), (w, 0), (0, 0)))[:, :S]
        mean = (c - prev) / jnp.minimum(count_base, float(w))[None, :, None]
        pooled.append(mean - uf[:, :, g])
    pooled = jnp.stack(pooled, axis=2).astype(u.dtype)
    mixed = jnp.einsum('bsgc,gcd->bsgd', pooled, w_grp).reshape(B, S, D_INNER) * scale
    return (mixed * jax.nn.silu(z)) @ w_out

def causal_depthwise_conv(x, w):
    return lax.conv_general_dilated(
        x, w[:, None, :].astype(x.dtype), window_strides=(1,),
        padding=[(CONV_WIDTH - 1, 0)], dimension_numbers=('NWC', 'WIO', 'NWC'),
        feature_group_count=x.shape[-1])

def conv_mixer(xn, w_in, conv_w, w_out):
    b, c, h, z = jnp.split(xn @ w_in, 4, axis=-1)
    y = b * causal_depthwise_conv(c * h, conv_w)
    return (y * jax.nn.silu(z)) @ w_out

def apply_rope(x, cos, sin):
    half = x.shape[-1] // 2
    x1, x2 = x[..., :half], x[..., half:]
    return jnp.concatenate([x1 * cos - x2 * sin, x2 * cos + x1 * sin], axis=-1).astype(x.dtype)

def causal_block_attention(q_nope, q_rope, k_nope, k_rope, v):
    B, S, H, _ = q_nope.shape
    nb = S // Q_BLOCK
    qn = q_nope.reshape(B, nb, Q_BLOCK, H, QK_NOPE_DIM).transpose(1, 0, 2, 3, 4)
    qr = q_rope.reshape(B, nb, Q_BLOCK, H, QK_ROPE_DIM).transpose(1, 0, 2, 3, 4)
    starts = jnp.arange(nb, dtype=jnp.int32) * Q_BLOCK
    key_idx = jnp.arange(S, dtype=jnp.int32)

    def one_block(args):
        qn_b, qr_b, start = args
        s = (jnp.einsum('bqhd,bkhd->bhqk', qn_b, k_nope).astype(jnp.float32)
             + jnp.einsum('bqhr,bkr->bhqk', qr_b, k_rope).astype(jnp.float32)) * ATTN_SCALE
        q_idx = start + jnp.arange(Q_BLOCK, dtype=jnp.int32)
        mask = key_idx[None, :] <= q_idx[:, None]
        s = jnp.where(mask[None, None], s, jnp.float32(-1e30))
        p = jax.nn.softmax(s, axis=-1).astype(v.dtype)
        return jnp.einsum('bhqk,bkhd->bqhd', p, v)

    o = lax.map(one_block, (qn, qr, starts))
    return o.transpose(1, 0, 2, 3, 4).reshape(B, S, H, V_HEAD_DIM)

def mla_mixer(xn, cos, sin, w_in, q_norm, w_q_up, kv_norm, w_kv_up, w_out):
    B, S, _ = xn.shape
    h = xn @ w_in
    q_lat, kv_lat, k_rope, z = jnp.split(
        h, [Q_LORA_RANK, Q_LORA_RANK + KV_LORA_RANK,
            Q_LORA_RANK + KV_LORA_RANK + QK_ROPE_DIM], axis=-1)
    q = (rms_norm(q_lat, q_norm) @ w_q_up).reshape(B, S, N_HEADS, QK_NOPE_DIM + QK_ROPE_DIM)
    q_nope = q[..., :QK_NOPE_DIM]
    q_rope = apply_rope(q[..., QK_NOPE_DIM:], cos[:, :, None, :], sin[:, :, None, :])
    kv = (rms_norm(kv_lat, kv_norm) @ w_kv_up).reshape(B, S, N_HEADS, QK_NOPE_DIM + V_HEAD_DIM)
    k_nope, v = kv[..., :QK_NOPE_DIM], kv[..., QK_NOPE_DIM:]
    k_rope = apply_rope(k_rope, cos, sin)
    o = causal_block_attention(q_nope, q_rope, k_nope, k_rope, v)
    return (o.reshape(B, S, D_INNER) * jax.nn.silu(z)) @ w_out

def first_inputs(seed: int = 0) -> dict:
    key = jax.random.key(seed)
    ks = jax.random.split(key, 20)

    def normal(k, shape, scale):
        return jax.random.normal(k, shape, jnp.float32) * scale

    def gain(k, shape):
        return 1.0 + 0.02 * jax.random.normal(k, shape, jnp.float32)

    x = normal(ks[0], (BATCH, SEQ, D_MODEL), 1.0)
    offset = jax.random.randint(ks[1], (BATCH, 1), 0, MAX_POS_OFFSET, dtype=jnp.int32)
    positions = (offset + jnp.arange(SEQ, dtype=jnp.int32)[None, :]).astype(jnp.int32)
    return {
        "x": x,
        "positions": positions,
        "pool_norm": gain(ks[2], (N_POOL, D_MODEL)),
        "pool_w_in": normal(ks[3], (N_POOL, D_MODEL, 2 * D_INNER), D_MODEL ** -0.5),
        "pool_w_grp": normal(ks[4], (N_POOL, N_POOL_GROUPS, POOL_GROUP, POOL_GROUP), POOL_GROUP ** -0.5),
        "pool_scale": gain(ks[5], (N_POOL, D_INNER)),
        "pool_w_out": normal(ks[6], (N_POOL, D_INNER, D_MODEL), D_INNER ** -0.5),
        "conv_norm": gain(ks[7], (N_CONV, D_MODEL)),
        "conv_w_in": normal(ks[8], (N_CONV, D_MODEL, 4 * D_INNER), D_MODEL ** -0.5),
        "conv_w": normal(ks[9], (N_CONV, CONV_WIDTH, D_INNER), CONV_WIDTH ** -0.5),
        "conv_w_out": normal(ks[10], (N_CONV, D_INNER, D_MODEL), D_INNER ** -0.5),
        "mla_norm": gain(ks[11], (N_MLA, D_MODEL)),
        "mla_w_in": normal(ks[12], (N_MLA, D_MODEL, MLA_IN_DIM), D_MODEL ** -0.5),
        "mla_q_norm": gain(ks[13], (N_MLA, Q_LORA_RANK)),
        "mla_w_q_up": normal(ks[14], (N_MLA, Q_LORA_RANK, N_HEADS * (QK_NOPE_DIM + QK_ROPE_DIM)), Q_LORA_RANK ** -0.5),
        "mla_kv_norm": gain(ks[15], (N_MLA, KV_LORA_RANK)),
        "mla_w_kv_up": normal(ks[16], (N_MLA, KV_LORA_RANK, N_HEADS * (QK_NOPE_DIM + V_HEAD_DIM)), KV_LORA_RANK ** -0.5),
        "mla_w_out": normal(ks[17], (N_MLA, D_INNER, D_MODEL), D_INNER ** -0.5),
        "final_norm": gain(ks[18], (D_MODEL,)),
    }

def first_block(x, positions, pool_norm, pool_w_in, pool_w_grp, pool_scale, pool_w_out,
              conv_norm, conv_w_in, conv_w, conv_w_out,
              mla_norm, mla_w_in, mla_q_norm, mla_w_q_up, mla_kv_norm, mla_w_kv_up, mla_w_out,
              final_norm):
    inv_freq = ROPE_BASE ** (-jnp.arange(0, QK_ROPE_DIM, 2, dtype=jnp.float32) / QK_ROPE_DIM)
    angles = positions.astype(jnp.float32)[..., None] * inv_freq
    cos, sin = jnp.cos(angles).astype(x.dtype), jnp.sin(angles).astype(x.dtype)

    for i in range(DEPTH):
        kind, j = i % N_MIXERS, i // N_MIXERS
        if kind == 0:
            xn = rms_norm(x, pool_norm[j])
            x = x + pool_mixer(xn, pool_w_in[j], pool_w_grp[j], pool_scale[j], pool_w_out[j])
        elif kind == 1:
            xn = rms_norm(x, conv_norm[j])
            x = x + conv_mixer(xn, conv_w_in[j], conv_w[j], conv_w_out[j])
        else:
            xn = rms_norm(x, mla_norm[j])
            x = x + mla_mixer(xn, cos, sin, mla_w_in[j], mla_q_norm[j], mla_w_q_up[j],
                              mla_kv_norm[j], mla_w_kv_up[j], mla_w_out[j])
    return rms_norm(x, final_norm)


DEPTH_2 = 1

HEAD_DIM = 64
SWA_HEADS = 4
SWA_KV_HEADS = 2
SWA_WINDOW = 128
SWA_BLOCK = 128
MOBA_HEADS = 4
MOBA_BLOCK = 256
MOBA_TOPK = 3
MOBA_QCHUNK = 64
DN_HEADS = 4
DN_HEAD_DIM = 128
DN_CONV = 4
DN_CHUNK = 64
D_FF = 2816
FFN_CONV = 3

NEG_INF = -1e30

SWA_Q = SWA_HEADS * HEAD_DIM
SWA_KV = SWA_KV_HEADS * HEAD_DIM
MOBA_W = MOBA_HEADS * HEAD_DIM
DN_W = DN_HEADS * DN_HEAD_DIM
MIX_WIDTH = SWA_Q + MOBA_W + DN_W
IN_SPLIT_SIZES = (SWA_Q, SWA_KV, SWA_KV, MOBA_W, MOBA_W, MOBA_W, 3 * DN_W, DN_W, DN_HEADS, DN_HEADS)
IN_WIDTH = SWA_Q + 2 * SWA_KV + 3 * MOBA_W + 4 * DN_W + 2 * DN_HEADS


def rms_norm_2(x, w):
    xf = x.astype(jnp.float32)
    y = xf * lax.rsqrt(jnp.mean(xf * xf, axis=-1, keepdims=True) + NORM_EPS)
    return (y * w.astype(jnp.float32)).astype(x.dtype)

def l2_norm(x):
    return x * lax.rsqrt(jnp.sum(x * x, axis=-1, keepdims=True) + NORM_EPS)

def alibi_slopes():
    n = SWA_HEADS + MOBA_HEADS
    s = 2.0 ** (-8.0 * jnp.arange(1, n + 1, dtype=jnp.float32) / n)
    return s[0::2], s[1::2]

def causal_depthwise_conv_2(x, w):
    K = w.shape[0]
    S = x.shape[1]
    xp = jnp.pad(x, ((0, 0), (K - 1, 0), (0, 0)))
    y = xp[:, 0:S] * w[0]
    for i in range(1, K):
        y = y + xp[:, i:i + S] * w[i]
    return y

def swa_sink_attention(q, k, v, sinks, slopes):
    B, S, Hq, d = q.shape
    Hkv = k.shape[2]
    G = Hq // Hkv
    nb = S // SWA_BLOCK
    qb = q.reshape(B, nb, SWA_BLOCK, Hkv, G, d)
    kb = k.reshape(B, nb, SWA_BLOCK, Hkv, d)
    vb = v.reshape(B, nb, SWA_BLOCK, Hkv, d)

    def with_prev(t):
        prev = jnp.pad(t, ((0, 0), (1, 0), (0, 0), (0, 0), (0, 0)))[:, :-1]
        return jnp.concatenate([prev, t], axis=2)

    kk, vv = with_prev(kb), with_prev(vb)
    scores = jnp.einsum('bnqhgd,bnshd->bnhgqs', qb, kk).astype(jnp.float32) * (d ** -0.5)
    rel = jnp.arange(SWA_BLOCK)[:, None] + SWA_BLOCK - jnp.arange(2 * SWA_BLOCK)[None, :]
    kpos = (jnp.arange(nb) * SWA_BLOCK - SWA_BLOCK)[:, None] + jnp.arange(2 * SWA_BLOCK)[None, :]
    valid = ((rel >= 0) & (rel < SWA_WINDOW))[None] & (kpos >= 0)[:, None, :]
    m = slopes.astype(jnp.float32).reshape(Hkv, G)[:, :, None, None]
    scores = scores - m * rel.astype(jnp.float32)
    scores = jnp.where(valid[None, :, None, None], scores, NEG_INF)
    sink = sinks.astype(jnp.float32).reshape(Hkv, G)[:, :, None, None]
    mx = jnp.maximum(scores.max(axis=-1, keepdims=True), sink)
    p = jnp.exp(scores - mx)
    denom = p.sum(axis=-1, keepdims=True) + jnp.exp(sink - mx)
    probs = (p / denom).astype(v.dtype)
    out = jnp.einsum('bnhgqs,bnshd->bnqhgd', probs, vv)
    return out.reshape(B, S, Hq, d)

def moba_attention(q, k, v, slopes):
    B, S, H, d = q.shape
    S_pad = -(-S // MOBA_BLOCK) * MOBA_BLOCK
    pad = ((0, 0), (0, S_pad - S), (0, 0), (0, 0))
    q, k, v = jnp.pad(q, pad), jnp.pad(k, pad), jnp.pad(v, pad)
    nblk = S_pad // MOBA_BLOCK
    topk = min(MOBA_TOPK, nblk)
    kb = k.reshape(B, nblk, MOBA_BLOCK, H, d).transpose(0, 3, 1, 2, 4)
    vb = v.reshape(B, nblk, MOBA_BLOCK, H, d).transpose(0, 3, 1, 2, 4)
    k_mean = kb.astype(jnp.float32).mean(axis=3)
    nq = S_pad // MOBA_QCHUNK
    q_chunks = q.reshape(B, nq, MOBA_QCHUNK, H, d).transpose(1, 0, 3, 2, 4)
    bi = jnp.arange(B)[:, None, None, None]
    hi = jnp.arange(H)[None, :, None, None]
    m = slopes.astype(jnp.float32)[None, :, None, None]
    scale = d ** -0.5
    offs = jnp.arange(MOBA_BLOCK)

    def chunk_attend(args):
        qc, c = args
        t = c * MOBA_QCHUNK + jnp.arange(MOBA_QCHUNK)
        own = (c * MOBA_QCHUNK) // MOBA_BLOCK
        gate = jnp.einsum('bhqd,bhnd->bhqn', qc.astype(jnp.float32), k_mean)
        gate = jnp.where(jnp.arange(nblk) < own, gate, NEG_INF)
        _, idx = lax.top_k(gate, topk)
        sel_ok = idx < own
        k_sel = kb[bi, hi, idx]
        v_sel = vb[bi, hi, idx]
        s_sel = jnp.einsum('bhqd,bhqrsd->bhqrs', qc, k_sel).astype(jnp.float32) * scale
        kpos_sel = idx[..., None] * MOBA_BLOCK + offs
        s_sel = s_sel - m[..., None] * (t[:, None, None] - kpos_sel).astype(jnp.float32)
        s_sel = jnp.where(sel_ok[..., None], s_sel, NEG_INF).reshape(B, H, MOBA_QCHUNK, topk * MOBA_BLOCK)
        k_own = lax.dynamic_index_in_dim(kb, own, axis=2, keepdims=False)
        v_own = lax.dynamic_index_in_dim(vb, own, axis=2, keepdims=False)
        rel_own = t[:, None] - (own * MOBA_BLOCK + offs)[None, :]
        s_own = jnp.einsum('bhqd,bhsd->bhqs', qc, k_own).astype(jnp.float32) * scale - m * rel_own.astype(jnp.float32)
        s_own = jnp.where(rel_own >= 0, s_own, NEG_INF)
        probs = jax.nn.softmax(jnp.concatenate([s_sel, s_own], axis=-1), axis=-1).astype(v.dtype)
        p_sel = probs[..., :topk * MOBA_BLOCK].reshape(B, H, MOBA_QCHUNK, topk, MOBA_BLOCK)
        p_own = probs[..., topk * MOBA_BLOCK:]
        return (jnp.einsum('bhqrs,bhqrsd->bqhd', p_sel, v_sel)
                + jnp.einsum('bhqs,bhsd->bqhd', p_own, v_own))

    out = lax.map(chunk_attend, (q_chunks, jnp.arange(nq)))
    out = out.transpose(1, 0, 2, 3, 4).reshape(B, S_pad, H, d)
    return out[:, :S]

def gated_delta_rule(q, k, v, g, beta):
    B, S, H, dk = q.shape
    dv = v.shape[-1]
    C = DN_CHUNK
    nc = S // C

    def chunks(t):
        t = t.reshape((B, nc, C, H) + t.shape[3:])
        return jnp.moveaxis(t, 3, 1)

    q = chunks(q) * (dk ** -0.5)
    k = chunks(k)
    v = chunks(v)
    g = jnp.cumsum(chunks(g), axis=-1)
    beta = chunks(beta)
    causal = jnp.tril(jnp.ones((C, C), dtype=bool))
    strict = jnp.tril(jnp.ones((C, C), dtype=bool), -1)
    gdiff = g[..., :, None] - g[..., None, :]
    decay = jnp.where(causal, jnp.exp(jnp.where(causal, gdiff, 0.0)), 0.0)
    k_beta = k * beta[..., None]
    L = jnp.where(strict, jnp.einsum('bhnid,bhnjd->bhnij', k_beta, k) * decay, 0.0)
    rhs = jnp.concatenate([v * beta[..., None], k_beta * jnp.exp(g)[..., None]], axis=-1)
    sol = lax.linalg.triangular_solve(L + jnp.eye(C, dtype=L.dtype), rhs, left_side=True,
                                      lower=True, unit_diagonal=True)
    u, w = sol[..., :dv], sol[..., dv:]
    a_intra = jnp.einsum('bhnid,bhnjd->bhnij', q, k) * decay
    q_dec = q * jnp.exp(g)[..., None]
    g_last = g[..., -1]
    k_dec = k * jnp.exp(g_last[..., None] - g)[..., None]

    def step(state, xs):
        w_c, u_c, qd_c, a_c, kd_c, gl_c = xs
        v_new = u_c - jnp.einsum('bhcd,bhde->bhce', w_c, state)
        o = jnp.einsum('bhcd,bhde->bhce', qd_c, state) + jnp.einsum('bhij,bhje->bhie', a_c, v_new)
        state = state * jnp.exp(gl_c)[..., None, None] + jnp.einsum('bhcd,bhce->bhde', kd_c, v_new)
        return state, o

    xs = (jnp.moveaxis(w, 2, 0), jnp.moveaxis(u, 2, 0), jnp.moveaxis(q_dec, 2, 0),
          jnp.moveaxis(a_intra, 2, 0), jnp.moveaxis(k_dec, 2, 0), jnp.moveaxis(g_last, 2, 0))
    state0 = jnp.zeros((B, H, dk, dv), jnp.float32)
    _, o = lax.scan(step, state0, xs)
    return o.transpose(1, 0, 3, 2, 4).reshape(B, S, H, dv)

def hybrid_token_mixer(h, w_in, swa_sinks, dn_conv_w, dn_a_log, dn_dt_bias, dn_norm, w_out,
                       slopes_swa, slopes_moba):
    B, S, _ = h.shape
    proj = h @ w_in
    split_at = np.cumsum(IN_SPLIT_SIZES)[:-1].tolist()
    qa, ka, va, qb, kb, vb, qkv_c, z_c, b_c, a_c = jnp.split(proj, split_at, axis=-1)
    o_a = swa_sink_attention(qa.reshape(B, S, SWA_HEADS, HEAD_DIM),
                             ka.reshape(B, S, SWA_KV_HEADS, HEAD_DIM),
                             va.reshape(B, S, SWA_KV_HEADS, HEAD_DIM), swa_sinks, slopes_swa)
    o_b = moba_attention(qb.reshape(B, S, MOBA_HEADS, HEAD_DIM), kb.reshape(B, S, MOBA_HEADS, HEAD_DIM),
                         vb.reshape(B, S, MOBA_HEADS, HEAD_DIM), slopes_moba)
    qkv_c = jax.nn.silu(causal_depthwise_conv_2(qkv_c, dn_conv_w)).astype(jnp.float32)
    qc, kc, vc = jnp.split(qkv_c, 3, axis=-1)
    qc = l2_norm(qc.reshape(B, S, DN_HEADS, DN_HEAD_DIM))
    kc = l2_norm(kc.reshape(B, S, DN_HEADS, DN_HEAD_DIM))
    vc = vc.reshape(B, S, DN_HEADS, DN_HEAD_DIM)
    beta = jax.nn.sigmoid(b_c.astype(jnp.float32))
    g = -jnp.exp(dn_a_log.astype(jnp.float32)) * jax.nn.softplus(a_c.astype(jnp.float32) + dn_dt_bias.astype(jnp.float32))
    o_c = gated_delta_rule(qc, kc, vc, g, beta)
    o_c = rms_norm_2(o_c, dn_norm) * jax.nn.silu(z_c.astype(jnp.float32).reshape(B, S, DN_HEADS, DN_HEAD_DIM))
    mixed = jnp.concatenate([o_a.reshape(B, S, SWA_Q), o_b.reshape(B, S, MOBA_W),
                             o_c.reshape(B, S, DN_W).astype(h.dtype)], axis=-1)
    return mixed @ w_out

def conv_glu_ffn(h, w_up, conv_w, conv_b, w_down):
    u = causal_depthwise_conv_2(h @ w_up, conv_w) + conv_b
    gate, up = jnp.split(u, 2, axis=-1)
    return (jax.nn.gelu(gate, approximate=True) * up) @ w_down

def second_inputs(seed: int = 0) -> dict:
    key = jax.random.key(seed)
    ks = jax.random.split(key, 16)
    f32 = jnp.float32

    def nrm(k, shape, scale):
        return jax.random.normal(k, shape, f32) * scale

    dt = jnp.exp(jax.random.uniform(ks[6], (DEPTH_2, DN_HEADS), f32)
                 * (math.log(0.1) - math.log(0.001)) + math.log(0.001))
    return {
        'x': nrm(ks[0], (BATCH, SEQ, D_MODEL), 1.0),
        'mix_pre_norm': 1.0 + nrm(ks[1], (DEPTH_2, D_MODEL), 0.05),
        'w_in': nrm(ks[2], (DEPTH_2, D_MODEL, IN_WIDTH), D_MODEL ** -0.5),
        'swa_sinks': nrm(ks[3], (DEPTH_2, SWA_HEADS), 0.5),
        'dn_conv_w': nrm(ks[4], (DEPTH_2, DN_CONV, 3 * DN_W), DN_CONV ** -0.5),
        'dn_a_log': jnp.log(jax.random.uniform(ks[5], (DEPTH_2, DN_HEADS), f32, 1.0, 16.0)),
        'dn_dt_bias': dt + jnp.log(-jnp.expm1(-dt)),
        'dn_norm': 1.0 + nrm(ks[7], (DEPTH_2, DN_HEAD_DIM), 0.05),
        'w_out': nrm(ks[8], (DEPTH_2, MIX_WIDTH, D_MODEL), MIX_WIDTH ** -0.5),
        'mix_post_norm': 1.0 + nrm(ks[9], (DEPTH_2, D_MODEL), 0.05),
        'ffn_pre_norm': 1.0 + nrm(ks[10], (DEPTH_2, D_MODEL), 0.05),
        'w_up': nrm(ks[11], (DEPTH_2, D_MODEL, 2 * D_FF), D_MODEL ** -0.5),
        'ffn_conv_w': nrm(ks[12], (DEPTH_2, FFN_CONV, 2 * D_FF), FFN_CONV ** -0.5),
        'ffn_conv_b': nrm(ks[13], (DEPTH_2, 2 * D_FF), 0.02),
        'w_down': nrm(ks[14], (DEPTH_2, D_FF, D_MODEL), D_FF ** -0.5),
        'ffn_post_norm': 1.0 + nrm(ks[15], (DEPTH_2, D_MODEL), 0.05),
    }

def second_block(x, mix_pre_norm, w_in, swa_sinks, dn_conv_w, dn_a_log, dn_dt_bias, dn_norm, w_out,
              mix_post_norm, ffn_pre_norm, w_up, ffn_conv_w, ffn_conv_b, w_down, ffn_post_norm):
    slopes_swa, slopes_moba = alibi_slopes()
    for l in range(DEPTH_2):
        h = rms_norm_2(x, mix_pre_norm[l])
        mix = hybrid_token_mixer(h, w_in[l], swa_sinks[l], dn_conv_w[l], dn_a_log[l], dn_dt_bias[l],
                                 dn_norm[l], w_out[l], slopes_swa, slopes_moba)
        x = x + rms_norm_2(mix, mix_post_norm[l])
        h = rms_norm_2(x, ffn_pre_norm[l])
        x = x + rms_norm_2(conv_glu_ffn(h, w_up[l], ffn_conv_w[l], ffn_conv_b[l], w_down[l]), ffn_post_norm[l])
    return x


def setup_inputs(seed=0):
    out = dict(first_inputs(seed))
    for name, value in second_inputs(seed + 1).items():
        if name != "x":
            out[name + "_2"] = value
    return out


def reference(
    x, positions, pool_norm, pool_w_in, pool_w_grp, pool_scale, pool_w_out, conv_norm,
    conv_w_in, conv_w, conv_w_out, mla_norm, mla_w_in, mla_q_norm, mla_w_q_up, mla_kv_norm,
    mla_w_kv_up, mla_w_out, final_norm, mix_pre_norm_2, w_in_2, swa_sinks_2, dn_conv_w_2,
    dn_a_log_2, dn_dt_bias_2, dn_norm_2, w_out_2, mix_post_norm_2, ffn_pre_norm_2, w_up_2,
    ffn_conv_w_2, ffn_conv_b_2, w_down_2, ffn_post_norm_2,
):
    x = first_block(
        x, positions, pool_norm, pool_w_in, pool_w_grp, pool_scale, pool_w_out, conv_norm,
        conv_w_in, conv_w, conv_w_out, mla_norm, mla_w_in, mla_q_norm, mla_w_q_up, mla_kv_norm,
        mla_w_kv_up, mla_w_out, final_norm,
    )
    return second_block(
        x, mix_pre_norm_2, w_in_2, swa_sinks_2, dn_conv_w_2, dn_a_log_2, dn_dt_bias_2,
        dn_norm_2, w_out_2, mix_post_norm_2, ffn_pre_norm_2, w_up_2, ffn_conv_w_2, ffn_conv_b_2,
        w_down_2, ffn_post_norm_2,
    )


_drawn_inputs = setup_inputs


def setup_inputs(seed=0):
    import zlib

    import numpy as np

    out = dict(_drawn_inputs(seed))
    spreads = {}
    factors = {'mla_norm': 8.0,
     'mla_q_norm': 8.0,
     'mla_kv_norm': 8.0,
     'swa_sinks_2': 64.0,
     'ffn_conv_b_2': 3.436}
    for name, (base, spread) in spreads.items():
        noise = np.random.default_rng([zlib.crc32(name.encode()), seed]).standard_normal(out[name].shape)
        drawn = base * np.exp(spread * noise) if base else spread * noise
        out[name] = __import__('jax').numpy.asarray(drawn.astype(out[name].dtype))
    for name, factor in factors.items():
        out[name] = (out[name] * factor).astype(out[name].dtype)
    return out
```

```python
import concourse.bass as bass
import concourse.mybir as mybir
from contextlib import ExitStack

F32 = mybir.dt.float32
F32R = mybir.dt.float32r
I32 = mybir.dt.int32
ALU = mybir.AluOpType
ACT = mybir.ActivationFunctionType
AX = mybir.AxisListType

P = 128
S = 512
D = 1024
DI = 2048
DT = D // P
IT = DI // P
FF = 2816
FT = FF // P
WINDOWS = (2, 4, 8, 16)
PAD = 16
CONV = 3
SCALE = (128 + 64) ** -0.5
EPS = 1e-6
TWO_PI = 6.283185307179586
TWO_PI_PARTS = (6.28125, 0.0019350051879882812, 3.0199159795074593e-07)
LEVELS = 6
CHUNK = 64
SLOPES = [2.0 ** -(i + 1) for i in range(8)]
SLOPES_SWA, SLOPES_MOBA = SLOPES[0::2], SLOPES[1::2]
FAR = 1e32
RING = 4
BANKS = 4
PHASES = ("pool0", "conv", "mla", "pool1", "final", "mixer", "ffn")

PARAMS = {}
_at = 0
for _name, _n in (("pool_norm0", DT), ("pool_norm1", DT), ("conv_norm", DT), ("mla_norm", DT), ("final_norm", DT),
                  ("mix_pre", DT), ("mix_post", DT), ("ffn_pre", DT), ("ffn_post", DT),
                  ("pool_scale0", IT), ("pool_scale1", IT), ("conv_w", CONV * IT), ("q_norm", 3), ("kv_norm", 2),
                  ("ffn_conv_w", CONV * 2 * FT), ("ffn_conv_b", 2 * FT), ("dn_conv", 4 * 12), ("dn_norm", 1),
                  ("sinks", 4), ("a_log", 1), ("dt_bias", 1)):
    PARAMS[_name] = _at
    _at += _n
NPARAMS = _at
CONSTS = {}
_at = 0
for _name, _n in (("ident", P), ("fold", P), ("causal", P), ("poolfix", 4 * PAD), ("freq", 1), ("phase", 1),
                  ("eps", 1)):
    CONSTS[_name] = _at
    _at += _n
NCONSTS = _at


CONSTS2 = {}
_at = 0
for _name, _n in (("levels", LEVELS * P), ("mask_t", P), ("dist", 4 * P), ("dist_swa", 2 * P)):
    CONSTS2[_name] = _at
    _at += _n
NCONSTS2 = _at


class Count:

    def __init__(self, start=0):
        self.n, self.i, self.per = start, None, 0

    def up(self, by=1):
        self.n += by
        return self.now()

    def now(self, ahead=0):
        return self.n + ahead if self.i is None else self.i * self.per + (self.n + ahead)

    def enter(self, i, per):
        self.i, self.per, self.first = i, per, self.n

    def leave(self, times):
        assert self.n == self.first + self.per, (self.n, self.first, self.per)
        self.n, self.i = self.first + self.per * times, None


class Steps:

    def __init__(self, names):
        self.names, self.value = names, {name: n + 1 for n, name in enumerate(names)}
        assert len(self.value) == len(names)
        self.made = 0

    def next(self, name):
        assert self.names[self.made] == name, (self.names[self.made], name)
        self.made += 1
        return self.made

    def __getitem__(self, name):
        return self.value[name]


def mixer_order():
    order = [("dve", "ydt"), ("act", "tanh"), ("pe", "colsum"), ("act", "e1"), ("act", "ln"), ("act", "nega"),
             ("act", "sqrt"), ("dve", "beta"), ("dve", "g"), ("dve", "rc"), ("pe", "rnt"), ("dve", "rn"),
             ("pe", "rowt"), ("dve", "cols"), ("act", "cexp"), ("dve", "cd"), ("act", "ckd")]
    per_head = [("pe", "bk"), ("dve", "kf"), ("pe", "bq"), ("dve", "qf"), ("pe", "bb"), ("dve", "kb"), ("pe", "bg"),
                ("dve", "dt"), ("act", "eg"), ("act", "egl"), ("act", "edt"), ("pe", "kt"), ("pe", "vt"),
                ("act", "vb"), ("dve", "kbe kd"), ("pe", "g1"), ("dve", "lt xt0 e1"), ("pe", "g2"), ("dve", "at qd"),
                ("pe", "x1"), ("act", "xc")]
    for l in range(1, LEVELS):
        per_head += [("pe", f"y{l}"), ("act", f"yc{l}")]
        if l < LEVELS - 1:
            per_head += [("dve", f"e{l + 1}")]
        per_head += [("pe", f"p{l}"), ("dve", f"xt{l}")]
    per_head += [("pe", "wt"), ("act", "nw")]
    for e, steps in per_head:
        order += [(e, (st, h)) for h in range(4) for st in steps.split()]
    for blk in range(4):
        order += [("pe", ("av", blk)), ("act", ("avc", blk))]
    n_blocks = 32
    slot = 0
    for c in range(8):
        order += [("pe", ("nv", c)), ("act", ("vn", c)), ("pe", ("o", c)), ("act", ("oc", c))]
        if c < 7:
            order += [("pe", ("su", c)), ("dve", ("st", c))]
        for _ in range(4 if c < 7 else 4 + 3):
            if slot < n_blocks:
                order += [("pe", ("s", slot)), ("dve", ("mx", slot)), ("act", ("ex", slot))]
            if 1 <= slot <= n_blocks:
                order += [("dve", ("nr", slot - 1))]
            if 2 <= slot <= n_blocks + 1:
                order += [("pe", ("t", slot - 2)), ("act", ("pc", slot - 2))]
            if slot >= 3:
                order += [("pe", ("pv", slot - 3))]
                if (slot - 3) % 8 == 7:
                    order += [("act", ("mc", (slot - 3) // 8))]
            slot += 1
    order += [("act", ("osq", h)) for h in range(4)]
    order += [("pe", "osum"), ("act", "osqrt"), ("dve", "orc"), ("pe", "ornt"), ("dve", "orn")]
    for h in range(4):
        order += [("pe", ("ob", h)), ("dve", ("on", h))]
    return order


class Rolled:

    def __init__(self, eng, times, pers):
        self.times, self.pers, self.loop = times, pers, eng.Fori(0, times)

    def __enter__(self):
        i = self.loop.__enter__()
        for c, per in self.pers.items():
            c.enter(i, per)
        return i

    def __exit__(self, *a):
        self.loop.__exit__(*a)
        if a[0] is None:
            for c in self.pers:
                c.leave(self.times)


def x_updates(phases):
    return sum(p in ("final", "mixer", "ffn") for p in phases)


def n_units(phases):
    per = {"pool0": 2 * IT + 2 * IT + IT + 4 * DT, "conv": 8 * IT + 4 * DT, "mla": 28 + 16 * 3 + 16 + 4 * DT,
           "final": 0, "mixer": 2 * 27 + 2 * DT, "ffn": 2 * 2 * FT + 6 * DT}
    per["pool1"] = per["pool0"]
    return sum(per[p] for p in phases) + RING


def program(nc, x_in, stream, params_in, consts_in, consts2_in, pos_in, out, phases):
    ctx = ExitStack()
    with ctx:
        def sb(name, shape, dt=F32, on=ctx):
            return on.enter_context(nc.sbuf_tensor(name, shape, dt))

        def sem(name):
            return ctx.enter_context(nc.semaphore(name))

        x = sb("x_res", [P, DT, S])
        late = ExitStack()
        x_mat = sb("x_mat", [P, 4, 4, P], F32, late)
        y_mat = sb("y_mat", [P, 4, 4, P], F32, late)
        l_mat = sb("l_mat", [P, 4, 4, P], F32, late)
        e_mat = sb("e_mat", [P, 4, 4, P], F32, late)
        d_mat = x_mat
        eg = y_mat
        v_tok = y_mat
        late.close()
        xh = sb("xh", [P, DT, S], F32R)
        xl = sb("xl", [P, DT, S], F32R)
        w_stage = sb("w_stage", [P, RING, S])
        w_hi = sb("w_hi", [P, RING, S], F32R)
        w_lo = sb("w_lo", [P, RING, S], F32R)
        params = sb("params_sb", [P, NPARAMS])
        consts = sb("consts_sb", [P, NCONSTS])
        ones = sb("ones", [P, P])
        rstd = sb("rstd", [P, S])
        std = sb("std", [P, S])
        sq = sb("sq", [P, 2, S])
        ssum = sb("ssum", [P, S])
        cs = sb("cs", [P, S])
        small = sb("small", [P, 16])
        prod = sb("prod", [P, S])
        spare = ExitStack()
        act_l = sb("act_l", [P, FT, S], F32R, spare)
        act_h = sb("act_h", [P, FT, S], F32R, spare)
        zone = ExitStack()
        upad = sb("upad", [P, 2, PAD + S], F32, zone)
        wsum = sb("wsum", [P, S], F32, zone)
        z4 = sb("z4", [P, 4, S], F32, zone)
        zone.close()
        zone = ExitStack()
        cb = sb("cb", [P, S], F32, zone)
        hb = sb("hb", [P, S], F32, zone)
        qpad = sb("qpad", [P, 2 + S], F32, zone)
        yb = sb("yb", [P, S], F32, zone)
        zb = sb("zb", [P, S], F32, zone)
        zone.close()
        zone = ExitStack()
        gpad = sb("gpad", [P, 2, 2 + S], F32, zone)
        yg = sb("yg", [P, 2, S], F32, zone)
        y = sb("y", [P, DT, S], F32, zone)
        zone.close()
        spare.close()

        over = ExitStack()
        og = sb("og", [P, IT, S], F32, over)
        lat = sb("lat", [P, 5, S], F32, over)
        lat_h = sb("lat_h", [P, 5, S], F32R, over)
        lat_l = sb("lat_l", [P, 5, S], F32R, over)
        rlat = sb("rlat", [P, S], F32, over)
        sum_kv = sb("sum_kv", [P, S], F32, over)
        k_rot = sb("k_rot", [P, S], F32, over)
        tk = sb("tk", [P, S], F32, over)
        qn = sb("qn", [P, 2, S], F32, over)
        qr = sb("qr", [P, 2, S], F32, over)
        kn = sb("kn", [P, 2, S], F32, over)
        vt = sb("vt", [P, 2, S], F32, over)
        pr = sb("pr", [P, 10, P], F32, over)
        pt = sb("pt", [P, 10, P], F32, over)
        zs = sb("zs", [P, 8, S], F32, over)
        over.close()
        over = ExitStack()
        pos_i = sb("pos_i", [P, S], I32, over)
        turns_i = sb("turns_i", [P, S], I32, over)
        turns = sb("turns", [P, S], F32, over)
        angle = sb("angle", [P, S], F32, over)
        over.close()

        over = ExitStack()
        mixed = sb("mixed", [P, DT, S], F32, over)
        consts2 = sb("consts2_sb", [P, NCONSTS2], F32, over)
        kf = sb("kf", [P, 4, S], F32, over)
        qf = sb("qf", [P, 4, S], F32, over)
        vf = sb("vf", [P, 4, S], F32, over)
        zc = sb("zc", [P, 4, S], F32, over)
        cpad = sb("cpad", [P, 4 + S], F32, over)
        rows = sb("rows", [P, S], F32, over)
        a_q = sb("a_q", [P, 2, S], F32, over)
        a_kv = sb("a_kv", [P, 2, S], F32, over)
        b_q = sb("b_q", [P, 2, S], F32, over)
        b_k = sb("b_k", [P, 2, S], F32, over)
        b_v = sb("b_v", [P, 2, S], F32, over)
        xt = sb("xt", [P, 4, 4, P], F32, over)
        squares_over = ExitStack()
        squares8 = sb("squares8", [P, 8, S], F32, squares_over)
        squares_over.close()
        vbeta = sb("vbeta", [P, 4, 4, P], F32, over)
        kdec = sb("kdec", [P, 4, 4, P], F32, over)
        reset = sb("reset", [P, S], F32, over)
        raw = sb("raw", [P, S], F32, over)
        state = sb("state", [P, 4, P], F32, over)
        vnew = sb("vnew", [P, S], F32, over)
        cy = sb("cy", [P, 2, S], F32, over)
        cols = sb("cols", [P, 4, 68], F32, over)
        rc = sb("rc", [P, 32], F32, over)
        ceg = sb("ceg", [P, 4, 4], F32, over)
        cbe = sb("cbe", [P, 4, 4], F32, over)
        ckd = sb("ckd", [P, 4, 4], F32, over)
        absy, rn = cy[:, 0, :], cy[:, 1, :]
        egl = sb("egl", [P, 4, 8], F32, over)
        soft = sb("soft", [P, 3, 4], F32, over)
        nega = sb("nega", [P, 1], F32, over)
        over.close()
        score_bufs = [x_mat[:, i, :, :] for i in range(3)]
        score_rows = [b.rearrange("p b k -> p (b k)") for b in score_bufs]
        osq = squares8

        proj = ctx.enter_context(nc.psum_tensor("proj", [P, BANKS, S], F32))
        aux = ctx.enter_context(nc.psum_tensor("aux", [P, 4, S], F32))

        loaded = [sem("loaded0"), sem("loaded1")]
        set_up = sem("set_up")
        x_loaded = [sem(f"x_loaded{h}") for h in range(4)]
        stored = sem("stored")
        stage_free = sem("stage_free")
        hi_done = sem("hi_done")
        slot_free = sem("slot_free")
        taken = sem("taken")
        sq_done = sem("sq_done")
        xh_done = sem("xh_done")
        xl_done = sem("xl_done")
        ssum_done = sem("ssum_done")
        stat_done = sem("stat_done")
        std_done = sem("std_done")
        prod_done = sem("prod_done")
        ah_done = sem("ah_done")
        al_done = sem("al_done")
        silu_done = sem("silu_done")
        gate_done = sem("gate_done")
        x_done = sem("x_done")
        pos_loaded = sem("pos_loaded")
        angle_done = sem("angle_done")
        cs_done = sem("cs_done")
        norm_done = sem("norm_done")
        lat_done = sem("lat_done")
        mul_done = sem("mul_done")
        lath_done = sem("lath_done")
        extra_done = sem("extra_done")
        k_rot_done = sem("k_rot_done")
        scores_done = sem("scores_done")
        bias_done = sem("bias_done")
        exp_done = sem("exp_done")
        probs_done = sem("probs_done")
        turned = sem("turned")
        pt_done = sem("pt_done")
        heads_done = sem("heads_done")
        og_done = sem("og_done")
        z_taken = sem("z_taken")
        ready = sem("ready")
        dve_step = sem("dve_step")
        consts2_loaded = sem("consts2_loaded")
        conv_done = sem("conv_done")
        heads_in = sem("heads_in")
        mix_pe, mix_dve, mix_act = sem("mix_pe"), sem("mix_dve"), sem("mix_act")

        order = mixer_order()
        PE_STEP, DVE_STEP, ACT_STEP = (Steps([name for eng, name in order if eng == e]) for e in ("pe", "dve", "act"))

        def banks(i):
            return proj[:, i, :] if i < BANKS else aux[:, i - BANKS, :]

        def blocks_of(ap):
            return ap.rearrange("p (b k) -> p b k", k=P)

        def level(l):
            return consts2[:, l * P:l * P + P].unsqueeze(1).broadcast_to([P, 4, P])

        def head_bank(h, i):
            return banks(2 * h + i)

        def attention_block(n):
            tile, qb, half = n // 8, n % 8 // 2, n % 2
            first = max(qb - 1, 0) if tile < 2 else 0
            return tile, qb, half, first * P, (qb + 1 - first) * P

        block = ctx.enter_context(nc.Block())

        def par(name, f):
            at = f + PARAMS[name]
            return params[:, bass.ds(at, 1)]

        def con(name, n=1, at=0):
            return consts[:, CONSTS[name] + at:CONSTS[name] + at + n]

        def split_after(n):
            return n + 1 < len(phases) and phases[n + 1] != "final"

        units = n_units(phases)
        assert units % RING in (0, 2)

        @block.sync
        def _(sp):
            for h in range(4):
                sp.dma_start(x[:, 2 * h:2 * h + 2, :], x_in[:, 2 * h:2 * h + 2, :]).then_inc(x_loaded[h], 16)
            def load(i, pair):
                sp.wait_ge(stage_free, i * RING + (2 * pair + 2))
                sp.dma_start(w_stage[:, 2 * pair:2 * pair + 2, :], stream[i * 2 + pair, :, :].rearrange("p (u n) -> p u n", u=2)).then_inc(loaded[pair], 16)

            with sp.Fori(0, units // RING) as i:
                load(i, 0)
                load(i, 1)
            if units % RING:
                load(units // RING, 0)
            if phases[-1] == "ffn":
                done = x_updates(phases)
                for h in range(4):
                    sp.wait_ge(x_done, DT * done - DT + 2 * h + 2)
                    sp.dma_start(out[:, 2 * h:2 * h + 2, :], x[:, 2 * h:2 * h + 2, :]).then_inc(stored, 16)
                sp.wait_ge(stored, 64)
            else:
                sp.wait_ge(x_done, DT * x_updates(phases) + 1)
                sp.dma_start(out, x[:, :, :]).then_inc(stored, 16)
                sp.wait_ge(stored, 16)

        @block.gpsimd
        def _(pool):
            pool.memset(ones[:, :], 1.0).then_inc(stage_free, RING)

            def lo(i, s):
                pool.wait_ge(hi_done, i * RING + (s + 1))
                pool.tensor_tensor(w_lo[:, s, :], w_stage[:, s, :], w_hi[:, s, :].bitcast(F32),
                                   ALU.subtract).then_inc(stage_free, 1)

            with pool.Fori(0, units // RING) as i:
                for s in range(RING):
                    lo(i, s)
            for s in range(units % RING):
                lo(units // RING, s)

        @block.tensor
        def _(pe):
            unit, tile = Count(), Count()
            al = Count()
            squares = Count()

            def products(bank, blocks, rhs, first_wait=None, hold=False):
                if bank is None:
                    o = aux[:, 0, :]
                else:
                    o = proj[:, bank, :]
                    pe.wait_ge(taken, tile.now(1))
                for b in range(blocks):
                    if b % 4 == 0:
                        pe.wait_ge(stage_free, unit.now(1 + RING))
                        slot = unit.n % RING
                    if first_wait is not None:
                        first_wait(b)
                    cols = slice(b % 4 * P, b % 4 * P + P)
                    hi, lo = rhs(b)
                    pe.matmul(o, w_hi[:, slot, cols], hi, start=(b == 0), stop=False)
                    pe.matmul(o, w_hi[:, slot, cols], lo, start=False, stop=False)
                    mm = pe.matmul(o, w_lo[:, slot, cols], hi, start=False, stop=(b == blocks - 1))
                    if (b % 4 == 3 or b == blocks - 1) and not hold:
                        mm.then_inc(slot_free, 1)
                        unit.up()
                if bank is not None:
                    tile.up()

            def of_x(k):
                return xh[:, k, :], xl[:, k, :]

            def of_act(k):
                return act_h[:, k, :], act_l[:, k, :]

            def project_in(tiles):
                products(tile.n % BANKS, 8, of_x, lambda k: pe.wait_ge(xl_done, 8 * x_norms[0] + k + 1))
                stats()
                for t in range(3):
                    products(tile.n % BANKS, 8, of_x)
                with Rolled(pe, tiles // 4 - 1, {unit: 8, tile: 4}):
                    for t in range(4):
                        products(tile.n % BANKS, 8, of_x)
                for t in range(tiles % 4):
                    products(tile.n % BANKS, 8, of_x)

            def project_out(k_tiles, per_tile, al_first):
                with Rolled(pe, DT // 4, {unit: 4 * per_tile, tile: 4}):
                    for t in range(4):
                        products(tile.n % BANKS, k_tiles, of_act, (lambda k: pe.wait_ge(al_done, al_first + k + 1)) if t == 0 else None)

            x_norms = [-1 if phases[0] == "final" else 0]

            def stats():
                pe.wait_ge(ssum_done, squares.up(DT))
                pe.matmul(aux[:, 0, :], ones[:, :], ssum[:, :], start=True, stop=True).then_inc(stat_done, 1)

            def latent_attention():
                for t in range(6):
                    products(tile.n % BANKS, 8, of_x,
                             (lambda k: pe.wait_ge(xl_done, 8 * x_norms[0] + k + 1)) if t == 0 else None)
                    if t == 0:
                        stats()
                squares.up(5)
                pe.wait_ge(norm_done, 1)
                pe.matmul(aux[:, 0, :], ones[:, :], ssum[:, :], start=True, stop=True).then_inc(stat_done, 1)
                pe.wait_ge(norm_done, 2)
                pe.matmul(aux[:, 1, :], ones[:, :], sum_kv[:, :], start=True, stop=True).then_inc(stat_done, 1)
                with Rolled(pe, 2, {unit: 8, tile: 4}):
                    for t in range(4):
                        products(tile.n % BANKS, 8, of_x)
                pe.wait_ge(norm_done, 3)
                pe.matmul(aux[:, 2, :], con("fold", P), tk[:, :], start=True, stop=True).then_inc(extra_done, 1)
                pe.wait_ge(lat_done, 5)
                of_lat = lambda first: (lambda k: (lat_h[:, first + k, :], lat_l[:, first + k, :]))

                def kv_tokens():
                    pe.wait_ge(taken, tile.now(1))
                    bank, slot = tile.n % BANKS, unit.n % RING
                    for blk in range(4):
                        toks = slice(blk * P, blk * P + P)
                        o = proj[:, bank, toks]
                        for k in range(2):
                            cols = slice((2 + k) * P, (3 + k) * P)
                            pe.matmul(o, lat_h[:, 3 + k, toks], w_hi[:, slot, cols], start=(k == 0), stop=False)
                            pe.matmul(o, lat_l[:, 3 + k, toks], w_hi[:, slot, cols], start=False, stop=False)
                            mm = pe.matmul(o, lat_h[:, 3 + k, toks], w_lo[:, slot, cols], start=False, stop=(k == 1))
                    mm.then_inc(slot_free, 1)
                    unit.up()
                    tile.up()

                def q_up():
                    products(tile.n % BANKS, 3, of_lat(0))

                def k_up():
                    products(tile.n % BANKS, 2, of_lat(3), hold=True)

                def scores(b, qb):
                    w = (qb + 1) * P
                    pe.wait_ge(exp_done, ex.now(1))
                    ex.up()
                    q, o = slice(qb * P, w), aux[:, 1 + qb % 2, 0:w]
                    pe.matmul(o, qn[:, b, q], kn[:, b, 0:w], start=True, stop=False)
                    pe.matmul(o, qr[:, b, q], k_rot[:, 0:w], start=False, stop=True).then_inc(scores_done, 1)

                def turn(qb):
                    pe.wait_ge(probs_done, tr.now(1))
                    pe.wait_ge(pt_done, tr.now(1))
                    tr.up()
                    at = qb * (qb + 1) // 2
                    for kb in range(qb + 1):
                        mm = pe.transpose(aux[:, 3, kb * P:kb * P + P], pr[:, at + kb, :], con("ident", P))
                    mm.then_inc(turned, 1)

                def head(b, nxt, z):
                    if nxt:
                        q_up()
                    turn(0)
                    scores(b, 2)
                    if nxt:
                        q_up()
                    turn(1)
                    scores(b, 3)
                    turn(2)
                    if nxt:
                        k_up()
                        kv_tokens()
                    if z:
                        pe.wait_ge(og_done, heads.now())
                        products(None, 8, of_x)
                        z_tiles.up()
                    turn(3)
                    if nxt:
                        first_scores(1 - b)
                    if z:
                        pe.wait_ge(z_taken, z_tiles.now(1))
                    pe.wait_ge(pt_done, tr.now(1))
                    for qb in range(4):
                        for kb in range(qb + 1):
                            mm = pe.matmul(aux[:, 0, qb * P:qb * P + P], vt[:, b, kb * P:kb * P + P],
                                           pt[:, qb * (qb + 1) // 2 + kb, :], start=(kb == 0), stop=(kb == qb))
                    mm.then_inc(heads_done, 1)
                    heads.up()

                def first_scores(b):
                    pe.wait_ge(taken, tile.now() + BANKS)
                    scores(b, 0)
                    scores(b, 1)

                ex, tr, z_tiles, heads = Count(), Count(), Count(), Count()
                q_up(); q_up(); k_up(); kv_tokens()
                first_scores(0)
                with Rolled(pe, 7, {unit: 8, tile: 8, ex: 8, tr: 8, z_tiles: 1, heads: 2}):
                    head(0, True, False)
                    head(1, True, True)
                head(0, True, False)
                head(1, False, True)

            def delta_heads():
                def made(ins, name):
                    ins.then_inc(mix_pe, 1)
                    PE_STEP.next(name)

                def spread_row(h, b, rows_of, n, row):
                    return pe.matmul(head_bank(h, b), consts[0:n, CONSTS["ident"] + row:CONSTS["ident"] + row + 1]
                                     .broadcast_to([n, P]), rows_of[0:n, :], start=True, stop=True)

                def per_block(h, b, stationary, moving, turn=False):
                    for blk in range(4):
                        o = blocks_of(head_bank(h, b))[:, blk, :]
                        if turn:
                            mm = pe.transpose(o, moving(blk), con("ident", P))
                        else:
                            mm = pe.matmul(o, stationary(blk), moving(blk), start=True, stop=True)
                    return mm

                heads = range(4)
                pe.wait_ge(mix_act, ACT_STEP["ckd"])
                for h in heads:
                    made(spread_row(h, 0, rn, 8, h), ("bk", h))
                for h in heads:
                    made(spread_row(h, 1, rn, 8, 4 + h), ("bq", h))
                for h in heads:
                    pe.wait_ge(mix_dve, DVE_STEP["kf", h])
                    made(spread_row(h, 0, rows, 64, h), ("bb", h))
                for h in heads:
                    pe.wait_ge(mix_dve, DVE_STEP["qf", h])
                    made(spread_row(h, 1, rows, 64, 32 + h), ("bg", h))
                for h in heads:
                    pe.wait_ge(mix_dve, DVE_STEP["kb", h])
                    made(per_block(h, 0, None, lambda blk: kf[:, h, blk * P:blk * P + P], turn=True), ("kt", h))
                for h in heads:
                    pe.wait_ge(mix_act, ACT_STEP["egl", h])
                    made(per_block(h, 1, None, lambda blk: vf[:, h, blk * P:blk * P + P], turn=True), ("vt", h))
                for h in heads:
                    pe.wait_ge(mix_dve, DVE_STEP["kd", h])
                    made(per_block(h, 0, lambda blk: kf[:, h, blk * P:blk * P + P],
                                   lambda blk: e_mat[:, h, blk, :]), ("g1", h))
                for h in heads:
                    pe.wait_ge(mix_act, ACT_STEP["vb", h])
                    made(per_block(h, 1, lambda blk: kf[:, h, blk * P:blk * P + P],
                                   lambda blk: qf[:, h, blk * P:blk * P + P]), ("g2", h))
                for h in heads:
                    pe.wait_ge(mix_dve, DVE_STEP["qd", h])
                    made(per_block(h, 0, None, lambda blk: xt[:, h, blk, :], turn=True), ("x1", h))
                for l in range(1, LEVELS):
                    for h in heads:
                        if l == 1:
                            pe.wait_ge(mix_dve, DVE_STEP["e1", h])
                            pe.wait_ge(mix_act, ACT_STEP["xc", h])
                        else:
                            pe.wait_ge(mix_dve, DVE_STEP[f"xt{l - 1}", h])
                        made(per_block(h, 1, lambda blk: e_mat[:, h, blk, :], lambda blk: x_mat[:, h, blk, :]), (f"y{l}", h))
                    for h in heads:
                        pe.wait_ge(mix_act, ACT_STEP[f"yc{l}", h])
                        mm = per_block(h, 0, lambda blk: y_mat[:, h, blk, :], lambda blk: xt[:, h, blk, :])
                        if l < LEVELS - 1:
                            mm = per_block(h, 1, lambda blk: xt[:, h, blk, :], lambda blk: y_mat[:, h, blk, :])
                        made(mm, (f"p{l}", h))
                for h in heads:
                    pe.wait_ge(mix_dve, DVE_STEP[f"xt{LEVELS - 1}", h])
                    made(per_block(h, 0, lambda blk: blocks_of(vf[:, h, :])[:, blk, :],
                                   lambda blk: xt[:, h, blk, :]), ("wt", h))

            def small_columns():
                pe.wait_ge(heads_in, 24)
                pe.wait_ge(taken, tile.now() + BANKS)
                for blk in range(4):
                    for i in range(8):
                        c = blk * 8 + i
                        mm = pe.matmul(banks(0)[:, c:c + 1], squares8[:, i, blk * P:blk * P + P], ones[:, 0:1],
                                       start=True, stop=True)
                mm.then_inc(mix_pe, 1)
                PE_STEP.next("colsum")
                pe.wait_ge(mix_dve, DVE_STEP["rc"])
                for blk in range(4):
                    mm = pe.transpose(banks(1)[0:8, blk * P:blk * P + P], rc[:, blk * 8:blk * 8 + 8], con("ident", P))
                mm.then_inc(mix_pe, 1)
                PE_STEP.next("rnt")
                for blk in range(4):
                    mm = pe.transpose(banks(2)[:, blk * 68:blk * 68 + 68], rows[0:68, blk * P:blk * P + P],
                                      consts[0:68, CONSTS["ident"]:CONSTS["ident"] + 68])
                mm.then_inc(mix_pe, 1)
                PE_STEP.next("rowt")
                pe.wait_ge(mix_dve, DVE_STEP["cd"])

            def chunk(c):
                blk, r = c // 2, CHUNK * (c % 2)
                toks = slice(c * CHUNK, c * CHUNK + CHUNK)
                if c == 0:
                    pe.wait_ge(mix_act, ACT_STEP["avc", 3])
                else:
                    pe.wait_ge(mix_dve, DVE_STEP["st", c - 1])
                    pe.wait_ge(mix_act, ACT_STEP["oc", c - 1])
                for h in range(4):
                    o = banks(0)[r:r + CHUNK, h * P:h * P + P]
                    mm = pe.matmul(o, xt[:, h, blk, r:r + CHUNK], vbeta[:, h, blk, :], start=(h == 0), stop=(c == 0),
                                   skip_group_check=True)
                    if c:
                        mm = pe.matmul(o, vf[:, h, toks], state[:, h, :], start=False, stop=True,
                                       skip_group_check=True)
                mm.then_inc(mix_pe, 1)
                PE_STEP.next(("nv", c))
                if c:
                    for h in range(4):
                        pe.matmul(banks(2)[:, h * CHUNK:h * CHUNK + CHUNK], state[:, h, :], qf[:, h, toks],
                                  start=(h == 0), stop=False, skip_group_check=True)
                pe.wait_ge(mix_act, ACT_STEP["vn", c])
                for h in range(4):
                    mm = pe.matmul(banks(2)[:, h * CHUNK:h * CHUNK + CHUNK], vnew[r:r + CHUNK, h * P:h * P + P],
                                   blocks_of(kf[:, h, :])[r:r + CHUNK, blk, r:r + CHUNK],
                                   start=(c == 0 and h == 0), stop=True, skip_group_check=True)
                mm.then_inc(mix_pe, 1)
                PE_STEP.next(("o", c))
                if c < 7:
                    for h in range(4):
                        mm = pe.matmul(banks(1)[:, h * P:h * P + P], kdec[r:r + CHUNK, h, blk, :],
                                       vnew[r:r + CHUNK, h * P:h * P + P], start=(h == 0), stop=True,
                                       skip_group_check=True)
                    mm.then_inc(mix_pe, 1)
                    PE_STEP.next(("su", c))

            def attend(slot):
                n = slot
                if n < 32:
                    tl, qb, half, first, w = attention_block(n)
                    head = 2 * (tl % 2) + half
                    part = slice(64 * (head // 2 if tl < 2 else half), 64 * (head // 2 if tl < 2 else half) + 64)
                    q, k = (a_q[part, head % 2, :], a_kv[part, 0, :]) if tl < 2 else (b_q[part, tl - 2, :], b_k[part, tl - 2, :])
                    if n >= 2:
                        pe.wait_ge(mix_dve, DVE_STEP["mx", n - 2])
                    pe.matmul(banks(3 + n % 2)[:, 0:w], q[:, qb * P:qb * P + P], k[:, first:first + w],
                              start=True, stop=True).then_inc(mix_pe, 1)
                    PE_STEP.next(("s", n))
                n = slot - 2
                if 0 <= n < 32:
                    w = attention_block(n)[4]
                    pe.wait_ge(mix_dve, DVE_STEP["nr", n])
                    if n:
                        pe.wait_ge(mix_act, ACT_STEP["pc", n - 1])
                    for kb in range(w // P):
                        mm = pe.transpose(banks(5)[:, kb * P:kb * P + P], score_bufs[n % 3][:, kb, :], con("ident", P))
                    mm.then_inc(mix_pe, 1)
                    PE_STEP.next(("t", n))
                n = slot - 3
                if 0 <= n < 32:
                    tl, qb, half, first, w = attention_block(n)
                    head = 2 * (tl % 2) + half
                    at = 64 * (head // 2) if tl < 2 else P + 64 * head
                    if n % 8 == 0 and tl >= 2:
                        pe.wait_ge(mix_act, ACT_STEP["mc", tl - 2])
                    pe.wait_ge(mix_act, ACT_STEP["pc", n])
                    for kb in range(w // P):
                        mm = pe.matmul(banks(6 + tl % 2)[64 * half:64 * half + 64, qb * P:qb * P + P],
                                       v_tok[:, first // P + kb, at // P, at % P:at % P + 64], e_mat[:, n % 2, kb, :],
                                       start=(kb == 0), stop=(kb == w // P - 1), skip_group_check=True)
                    mm.then_inc(mix_pe, 1)
                    PE_STEP.next(("pv", n))

            def hybrid_mixer():
                project_in(27)
                small_columns()
                delta_heads()
                pe.wait_ge(mix_act, ACT_STEP["nw", 3])
                for blk in range(4):
                    if blk >= 2:
                        pe.wait_ge(mix_act, ACT_STEP["avc", blk - 2])
                    for i, v in enumerate((a_kv[:, 1, :], b_v[:, 0, :], b_v[:, 1, :])):
                        mm = pe.transpose(banks(4 * (blk % 2) + 1)[:, i * P:i * P + P], v[:, blk * P:blk * P + P], con("ident", P))
                    mm.then_inc(mix_pe, 1)
                    PE_STEP.next(("av", blk))
                slot = 0
                for c in range(8):
                    chunk(c)
                    for _ in range(4 if c < 7 else 7):
                        attend(slot)
                        slot += 1
                pe.wait_ge(mix_act, ACT_STEP["osq", 3])
                for blk in range(4):
                    for h in range(4):
                        mm = pe.matmul(banks(0)[:, blk * 4 + h:blk * 4 + h + 1], osq[:, h, blk * P:blk * P + P], ones[:, 0:1],
                                       start=True, stop=True)
                mm.then_inc(mix_pe, 1)
                PE_STEP.next("osum")
                pe.wait_ge(mix_dve, DVE_STEP["orc"])
                for blk in range(4):
                    mm = pe.transpose(banks(1)[0:4, blk * P:blk * P + P], rc[:, blk * 4:blk * 4 + 4], con("ident", P))
                mm.then_inc(mix_pe, 1)
                PE_STEP.next("ornt")
                for h in range(4):
                    pe.wait_ge(mix_dve, DVE_STEP["orn"] if h < 2 else DVE_STEP["on", h - 2])
                    pe.matmul(banks(2 + h % 2), consts[0:4, CONSTS["ident"] + h:CONSTS["ident"] + h + 1]
                              .broadcast_to([4, P]), rn[0:4, :], start=True, stop=True).then_inc(mix_pe, 1)
                    PE_STEP.next(("ob", h))

            pe.wait_ge(stage_free, RING)
            if phases[0] == "final":
                stats()
            for n, ph in enumerate(phases):
                if ph.startswith("pool"):
                    project_in(IT)
                    with Rolled(pe, 4, {unit: 12, tile: 8}) as g:
                        for t in range(4):
                            products(tile.n % BANKS, 8, of_x)
                        for t in range(4):
                            products(tile.n % BANKS, 4, lambda c: (act_h[:, g * 4 + (4 + c), :], act_l[:, g * 4 + (4 + c), :]),
                                     (lambda c: pe.wait_ge(al_done, al.n + IT)) if t == 0 else None)
                    project_out(IT, 4, al.n + IT)
                    al.up(2 * IT)
                if ph == "conv":
                    project_in(4 * IT)
                    project_out(IT, 4, al.n)
                    al.up(IT)
                if ph == "mla":
                    latent_attention()
                    project_out(IT, 4, al.n)
                    al.up(IT)
                if ph == "mixer":
                    hybrid_mixer()
                    project_out(DT, 2, al.n)
                    al.up(DT)
                    stats()
                if ph == "ffn":
                    project_in(2 * FT)
                    project_out(FT, 6, al.n)
                    al.up(FT)
                    stats()
                if split_after(n):
                    x_norms[0] += 1
                elif ph not in ("mixer", "ffn"):
                    stats()

        @block.scalar
        def _(act):
            unit, tile = Count(), Count()
            sqs, hs, stds, als, prods, silus, gates, xs = (Count() for _ in range(8))

            def his(n):
                for _ in range(n):
                    u = unit.n
                    pair = (u // 2) % 2
                    value = 16 * (u // RING + 1)
                    if unit.i is not None:
                        value = unit.i * (unit.per // RING * 16) + value
                    act.wait_ge(loaded[pair], value)
                    act.wait_ge(slot_free, unit.now(1))
                    act.activation(w_hi[:, u % RING, :], w_stage[:, u % RING, :], ACT.Copy).then_inc(hi_done, 1)
                    unit.up()

            def square(of):
                if sqs.n > 1:
                    act.wait_ge(ssum_done, sqs.now() - 1)
                act.activation(sq[:, sqs.n % 2, :], of, ACT.Square).then_inc(sq_done, 1)
                sqs.up()

            def residual_tile(f, gain):
                square(x[:, f, :])
                if gain:
                    act.activation(xh[:, f, :], x[:, f, :], ACT.Identity, scale=par(gain, f)).then_inc(xh_done, 1)
                    hs.up()

            def deviation():
                stds.up()
                act.wait_ge(stat_done, stds.n)
                act.activation(std[:, :], aux[:, 0, :], ACT.Sqrt, bias=con("eps"), scale=1.0 / D).then_inc(std_done, 1)

            def out_tiles(per_tile, gain, of=x):
                with Rolled(act, DT // 4, {unit: 4 * per_tile, tile: 4, sqs: 4, hs: 4 if gain else 0}) as i:
                    for t in range(4):
                        his(per_tile)
                        act.wait_ge(taken, tile.up() + BANKS)
                        if of is x:
                            residual_tile(i * 4 + t, gain)
                        else:
                            square(of[:, i * 4 + t, :])
                deviation()

            def updated_tiles(gain):
                for f in range(DT):
                    act.wait_ge(x_done, xs.up())
                    residual_tile(f, gain)
                deviation()

            def operand(slot, wait, value):
                act.wait_ge(wait, value)
                act.activation(act_h[:, slot, :], prod[:, :], ACT.Copy).then_inc(ah_done, 1)

            def latent_attention(gain):
                act.dma_start(pos_i[:, :], pos_in).then_inc(pos_loaded, 16)
                for t in range(5):
                    his(2)
                    if t == 3:
                        act.wait_ge(angle_done, 1)
                        act.activation(cs[:, :], angle[:, :], ACT.Sin).then_inc(cs_done, 1)
                    act.wait_ge(taken, tile.up() + BANKS)
                    square(lat[:, t, :])
                his(2)
                tile.up()
                his(2)
                for bank, n in ((0, 384), (1, 256)):
                    stds.up()
                    act.wait_ge(stat_done, stds.n)
                    if bank:
                        act.wait_ge(norm_done, 4)
                    act.activation(std[:, :], aux[:, bank, :], ACT.Sqrt, bias=con("eps"), scale=1.0 / n).then_inc(std_done, 1)
                for f in range(5):
                    if f in (1, 3):
                        his(2)
                    act.wait_ge(mul_done, f + 1)
                    gain_f = par("q_norm", f) if f < 3 else par("kv_norm", f - 3)
                    act.activation(lat_h[:, f, :], lat[:, f, :], ACT.Identity, scale=gain_f).then_inc(lath_done, 1)
                his(2)
                for t in range(8):
                    if t >= 4:
                        his(2)
                    act.wait_ge(taken, tile.up() + BANKS)
                    act.activation(zs[:, t, :], zs[:, t, :], ACT.Silu).then_inc(silu_done, 1)
                    silus.up()
                his(3)
                tile.up(4)

                def expo(qb):
                    at, n = qb * (qb + 1) // 2, qb + 1
                    act.wait_ge(bias_done, es.up())
                    act.activation(pr[:, at:at + n, :], aux[:, 1 + qb % 2, 0:n * P].rearrange("p (b k) -> p b k", k=P), ACT.Exp,
                                   bias=small[:, 4 + qb:5 + qb], scale=SCALE,
                                   accum_out=small[:, 8 + qb:9 + qb]).then_inc(exp_done, 1)

                def head(nxt, z):
                    if nxt:
                        his(1)
                    expo(2)
                    if nxt:
                        his(1)
                    expo(3)
                    if nxt:
                        his(1)
                        tile.up(4)
                    if z is not None:
                        his(2)
                        act.wait_ge(z_taken, zts.up() + 1)
                        act.activation(zs[:, z, :], zs[:, z, :], ACT.Silu).then_inc(silu_done, 1)
                        silus.up()
                    if nxt:
                        expo(0)
                        expo(1)

                es, zts = Count(), Count()
                expo(0)
                expo(1)
                with Rolled(act, 7, {unit: 8, tile: 8, es: 8, zts: 1, silus: 1}) as i:
                    head(True, None)
                    head(True, i)
                head(True, None)
                head(False, 7)
                for k in range(IT):
                    if k == 0:
                        act.wait_ge(og_done, IT)
                    act.activation(act_h[:, k, :], og[:, k, :], ACT.Copy).then_inc(ah_done, 1)

            def hybrid_mixer():
                act.dma_start(consts2[:, :], consts2_in).then_inc(consts2_loaded, 16)
                ins = Count()

                def conv_tile(n, to, square_to=None):
                    act.wait_ge(conv_done, n + 1)
                    act.activation(to, cy[:, n % 2, :], ACT.Silu).then_inc(heads_in, 1)
                    ins.up()
                    if square_to is not None:
                        act.wait_ge(heads_in, ins.now())
                        act.activation(square_to, to, ACT.Square).then_inc(heads_in, 1)
                        ins.up()

                for i in range(8):
                    his(2)
                    tile.up()
                    conv_tile(i, kf[:, i, :] if i < 4 else qf[:, i - 4, :], squares8[:, i, :])
                his(2)
                tile.up()
                for i in range(4):
                    his(2)
                    tile.up()
                    conv_tile(8 + i, vf[:, i, :])
                his(20)
                tile.up(10)
                for i in range(4):
                    his(2)
                    act.wait_ge(taken, tile.up() + BANKS)
                    act.activation(zc[:, i, :], zc[:, i, :], ACT.Silu).then_inc(heads_in, 1)

                def made(i, name):
                    i.then_inc(mix_act, 1)
                    act.wait_ge(mix_act, ACT_STEP.next(name))

                act.wait_ge(mix_dve, DVE_STEP["ydt"])
                made(act.activation(raw[0:4, :], raw[0:4, :], ACT.Tanh, scale=0.5), "tanh")
                made(act.activation(absy[32:36, :], absy[32:36, :], ACT.Exp, scale=-1.0), "e1")
                made(act.activation(absy[32:36, :], absy[32:36, :], ACT.Ln, bias=ones[32:36, 0:1]), "ln")
                made(act.activation(nega[32:36, :], params[32:36, PARAMS["a_log"]:PARAMS["a_log"] + 1], ACT.Exp), "nega")
                act.wait_ge(mix_pe, PE_STEP["colsum"])
                made(act.activation(rc[:, :], banks(0)[:, 0:32], ACT.Sqrt, bias=con("eps")), "sqrt")
                act.wait_ge(mix_dve, DVE_STEP["cols"])
                made(act.activation(ceg[:, :, :], cols[:, :, 32:36], ACT.Exp), "cexp")
                act.wait_ge(mix_dve, DVE_STEP["cd"])
                made(act.activation(ckd[:, :, :], ckd[:, :, :], ACT.Exp), "ckd")
                heads = range(4)
                for h in heads:
                    act.wait_ge(mix_dve, DVE_STEP["dt", h])
                    made(act.activation(eg[:, h, :, :], blocks_of(head_bank(h, 1)), ACT.Exp), ("eg", h))
                for h in heads:
                    made(act.activation(egl[:, h, :], head_bank(h, 1)[:, CHUNK - 1::CHUNK], ACT.Exp), ("egl", h))
                for h in heads:
                    made(act.activation(d_mat[:, h, :, :], d_mat[:, h, :, :], ACT.Exp), ("edt", h))
                for h in heads:
                    act.wait_ge(mix_pe, PE_STEP["vt", h])
                    for blk in range(4):
                        ins = act.activation(vbeta[:, h, blk, :], head_bank(h, 1)[:, blk * P:blk * P + P], ACT.Copy,
                                             scale=cols[:, blk, h:h + 1])
                    made(ins, ("vb", h))
                for h in heads:
                    act.wait_ge(mix_pe, PE_STEP["x1", h])
                    made(act.activation(x_mat[:, h, :, :], blocks_of(head_bank(h, 0)), ACT.Copy), ("xc", h))
                for l in range(1, LEVELS):
                    for h in heads:
                        act.wait_ge(mix_pe, PE_STEP[f"y{l}", h])
                        made(act.activation(y_mat[:, h, :, :], blocks_of(head_bank(h, 1)), ACT.Copy), (f"yc{l}", h))
                for h in heads:
                    act.wait_ge(mix_pe, PE_STEP["wt", h])
                    made(act.activation(vf[:, h, :], head_bank(h, 0), ACT.Copy, scale=-1.0), ("nw", h))
                for blk in range(4):
                    act.wait_ge(mix_pe, PE_STEP["av", blk])
                    made(act.activation(v_tok[:, blk, 0:3, :], banks(4 * (blk % 2) + 1)[:, 0:3 * P].rearrange("p (b k) -> p b k", k=P),
                                        ACT.Copy), ("avc", blk))

                def attend(slot):
                    n = slot
                    if n < 32:
                        tl, qb, half, first, w = attention_block(n)
                        s = score_rows[n % 3][:, 0:w]
                        act.wait_ge(mix_dve, DVE_STEP["mx", n])
                        e = act.activation(s, s, ACT.Exp, bias=soft[:, n % 3, 0:1], accum_out=soft[:, n % 3, 1:2])
                        if tl < 2:
                            head = PARAMS["sinks"] + 2 * tl + half
                            e = act.activation(soft[:, n % 3, 2:3], params[:, head:head + 1], ACT.Exp, bias=soft[:, n % 3, 0:1])
                        made(e, ("ex", n))
                    n = slot - 2
                    if 0 <= n < 32:
                        w = attention_block(n)[4]
                        act.wait_ge(mix_pe, PE_STEP["t", n])
                        made(act.activation(e_mat[:, n % 2, 0:w // P, :], blocks_of(banks(5)[:, 0:w]), ACT.Copy), ("pc", n))
                    n = slot - 3
                    if 0 <= n < 32 and n % 8 == 7:
                        act.wait_ge(mix_pe, PE_STEP["pv", n])
                        made(act.activation(mixed[:, n // 8, :], banks(6 + n // 8 % 2), ACT.Copy), ("mc", n // 8))

                slot = 0
                for c in range(8):
                    r = CHUNK * (c % 2)
                    act.wait_ge(mix_pe, PE_STEP["nv", c])
                    made(act.activation(vnew[r:r + CHUNK, :], banks(0)[r:r + CHUNK, :], ACT.Copy), ("vn", c))
                    act.wait_ge(mix_pe, PE_STEP["o", c])
                    made(act.activation(mixed[:, 4:8, c * CHUNK:c * CHUNK + CHUNK],
                                        banks(2)[:, 0:4 * CHUNK].rearrange("p (h k) -> p h k", k=CHUNK), ACT.Copy), ("oc", c))
                    for _ in range(4 if c < 7 else 7):
                        attend(slot)
                        slot += 1
                for h in range(4):
                    made(act.activation(osq[:, h, :], mixed[:, 4 + h, :], ACT.Square), ("osq", h))
                act.wait_ge(mix_pe, PE_STEP["osum"])
                made(act.activation(rc[:, 0:16], banks(0)[:, 0:16], ACT.Sqrt, bias=con("eps"), scale=1.0 / P), "osqrt")
                act.wait_ge(mix_dve, DVE_STEP["on", 3])
                for k in range(DT):
                    act.activation(act_h[:, k, :], mixed[:, k, :], ACT.Copy).then_inc(ah_done, 1)

            act.dma_start(params[:, :], params_in).then_inc(set_up, 16)
            act.dma_start(consts[:, :], consts_in).then_inc(set_up, 16)
            act.wait_ge(set_up, 32)
            for f in range(DT):
                act.wait_ge(x_loaded[f // 2], 16)
                residual_tile(f, phases[0] != "final" and NORM_OF[phases[0]])
                if f == 3:
                    his(2)
                if f == 6:
                    his(2)
            deviation()
            for n, ph in enumerate(phases):
                nxt = NORM_OF[phases[n + 1]] if split_after(n) else None
                if ph.startswith("pool"):
                    with Rolled(act, 4, {unit: 8, tile: 4, prods: 4}) as g:
                        for t in range(4):
                            his(2)
                            tile.up()
                            operand(g * 4 + (4 + t), prod_done, prods.up())
                    with Rolled(act, 4, {unit: 12, tile: 8, silus: 4}) as g:
                        for t in range(4):
                            his(2)
                            act.wait_ge(taken, tile.up() + BANKS)
                            act.activation(z4[:, t, :], z4[:, t, :], ACT.Silu).then_inc(silu_done, 1)
                            silus.up()
                        for t in range(4):
                            his(1)
                            operand(g * 4 + t, taken, tile.up() + BANKS)
                    out_tiles(4, nxt)
                if ph == "conv":
                    with Rolled(act, IT, {unit: 8, tile: 4, silus: 1, prods: 1}) as f:
                        for t in range(4):
                            his(2)
                            tile.up()
                        act.wait_ge(taken, tile.now() + BANKS)
                        act.activation(zb[:, :], zb[:, :], ACT.Silu).then_inc(silu_done, 1)
                        silus.up()
                        operand(f, prod_done, prods.up())
                    out_tiles(4, nxt)
                if ph == "mla":
                    latent_attention(nxt)
                    out_tiles(4, nxt)
                if ph == "final":
                    updated_tiles(nxt)
                if ph == "mixer":
                    hybrid_mixer()
                    out_tiles(2, None, of=y)
                    if nxt:
                        updated_tiles(nxt)
                if ph == "ffn":
                    with Rolled(act, FT // 2, {unit: 8, tile: 4, gates: 2, silus: 2, prods: 2}) as i:
                        for t in range(2):
                            his(4)
                            tile.up(2)
                            act.wait_ge(gate_done, gates.up())
                            act.activation(yg[:, 0, :], yg[:, 0, :], ACT.Gelu_apprx_tanh).then_inc(silu_done, 1)
                            silus.up()
                            operand(i * 2 + t, prod_done, prods.up())
                    out_tiles(6, None, of=y)

        @block.vector
        def _(dve):
            unit, tile, step = Count(), Count(), Count()
            sqs, hs, stds, prods, als, silus, gates, xs = (Count() for _ in range(8))

            def link(ins):
                ins.then_inc(dve_step, 1)
                dve.wait_ge(dve_step, step.up())

            def bank(n_units):
                unit.up(n_units)
                dve.wait_ge(slot_free, unit.now() + RING)
                return proj[:, tile.n % BANKS, :]

            def take(ins):
                ins.then_inc(taken, 1)
                dve.wait_ge(taken, tile.up() + BANKS)

            def add_square():
                dve.wait_ge(sq_done, sqs.up())
                dve.tensor_tensor(ssum[:, :], ssum[:, :], sq[:, (sqs.n - 1) % 2, :], ALU.add).then_inc(ssum_done, 1)
                dve.wait_ge(ssum_done, sqs.now())

            def residual_tile(f, gain):
                add_square()
                if gain:
                    dve.wait_ge(xh_done, hs.up())
                    dve.scalar_tensor_tensor(xl[:, f, :], x[:, f, :], par(gain, f), xh[:, f, :].bitcast(F32),
                                             ALU.mult, ALU.subtract).then_inc(xl_done, 1)

            def deviation():
                stds.up()
                dve.wait_ge(std_done, stds.n)
                link(dve.reciprocal(rstd[:, :], std[:, :]))
                link(dve.memset(ssum[:, :], 0.0))

            def out_tiles(per_tile, gain, of=x):
                with Rolled(dve, DT // 4, {unit: 4 * per_tile, tile: 4, sqs: 4, hs: 4 if gain else 0}) as i:
                    for t in range(4):
                        f = i * 4 + t
                        b = bank(per_tile)
                        if of is x:
                            take(dve.tensor_tensor(x[:, f, :], b, x[:, f, :], ALU.add))
                            residual_tile(f, gain)
                        else:
                            take(dve.tensor_copy(of[:, f, :], b))
                            add_square()
                deviation()

            def add_normed(post, gain):
                for f in range(DT):
                    link(dve.scalar_tensor_tensor(y[:, f, :], y[:, f, :], par(post, f), rstd[:, :],
                                                  ALU.mult, ALU.mult))
                    dve.tensor_tensor(x[:, f, :], x[:, f, :], y[:, f, :], ALU.add).then_inc(x_done, 1)
                    dve.wait_ge(x_done, xs.up())
                    if gain and f:
                        residual_tile(f - 1, gain)
                if gain:
                    residual_tile(DT - 1, gain)
                if gain:
                    deviation()

            def rest(slot):
                als.up()
                dve.wait_ge(ah_done, als.now())
                dve.tensor_tensor(act_l[:, slot, :], prod[:, :], act_h[:, slot, :].bitcast(F32),
                                  ALU.subtract).then_inc(al_done, 1)
                dve.wait_ge(al_done, als.now())

            def angles():
                dve.wait_ge(pos_loaded, 16)
                link(dve.tensor_copy(turns[:, :], pos_i[:, :]))
                link(dve.tensor_scalar(angle[:, :], turns[:, :], con("freq"), None, ALU.mult))
                link(dve.tensor_scalar(turns_i[:, :], angle[:, :], con("phase"), 1.0 / TWO_PI, ALU.add, ALU.mult))
                link(dve.tensor_copy(turns[:, :], turns_i[:, :]))
                for part in TWO_PI_PARTS:
                    link(dve.scalar_tensor_tensor(angle[:, :], turns[:, :], -part, angle[:, :], ALU.mult, ALU.add))
                link(dve.tensor_scalar(angle[:, :], angle[:, :], con("phase"), 3.1415925, ALU.add, ALU.min))
                dve.tensor_scalar(angle[:, :], angle[:, :], -3.1415925, None, ALU.max).then_inc(angle_done, 1)

            def latent_attention():
                for t in range(5):
                    take(dve.tensor_tensor(lat[:, t, :], bank(2), rstd[:, :], ALU.mult))
                    dve.wait_ge(sq_done, sqs.up())
                    total = ssum if t < 3 else sum_kv
                    if t == 3:
                        dve.tensor_copy(total[:, :], sq[:, (sqs.n - 1) % 2, :]).then_inc(ssum_done, 1)
                    else:
                        dve.tensor_tensor(total[:, :], total[:, :], sq[:, (sqs.n - 1) % 2, :], ALU.add).then_inc(ssum_done, 1)
                    dve.wait_ge(ssum_done, sqs.now())
                    if t in (2, 4):
                        dve.memset(small[:, 0:1], 0.0).then_inc(norm_done, 1)
                        dve.wait_ge(norm_done, 1 if t == 2 else 2)
                    if t == 1:
                        angles()
                take(dve.tensor_tensor(tk[:, :], bank(2), rstd[:, :], ALU.mult))
                dve.wait_ge(cs_done, 1)
                dve.tensor_tensor(tk[:, :], tk[:, :], cs[:, :], ALU.mult).then_inc(norm_done, 1)
                for part, fs in enumerate((range(3), range(3, 5))):
                    stds.up()
                    dve.wait_ge(std_done, stds.n)
                    r = dve.reciprocal(rlat[:, :], std[:, :])
                    if part == 0:
                        r.then_inc(norm_done, 1)
                        dve.wait_ge(norm_done, 4)
                    else:
                        link(r)
                    for f in fs:
                        dve.tensor_tensor(lat[:, f, :], lat[:, f, :], rlat[:, :], ALU.mult).then_inc(mul_done, 1)
                        dve.wait_ge(mul_done, f + 1)
                link(dve.memset(ssum[:, :], 0.0))
                for f in range(5):
                    gain_f = par("q_norm", f) if f < 3 else par("kv_norm", f - 3)
                    dve.wait_ge(lath_done, f + 1)
                    dve.scalar_tensor_tensor(lat_l[:, f, :], lat[:, f, :], gain_f, lat_h[:, f, :].bitcast(F32),
                                             ALU.mult, ALU.subtract).then_inc(lat_done, 1)
                for t in range(8):
                    take(dve.tensor_tensor(zs[:, t, :], bank(2), rstd[:, :], ALU.mult))
                dve.wait_ge(extra_done, 1)
                dve.tensor_copy(k_rot[:, :], aux[:, 2, :]).then_inc(z_taken, 1)
                dve.wait_ge(z_taken, 1)

                def take_qn(b):
                    take(dve.tensor_copy(qn[:, b, :], bank(1)))

                def take_qr(b):
                    take(dve.tensor_tensor(qr[:, b, :], bank(1), cs[:, :], ALU.mult))

                def take_kn(b):
                    take(dve.tensor_copy(kn[:, b, :], bank(1)))

                def take_vt(b):
                    take(dve.tensor_copy(vt[:, b, :], bank(0)))

                def row_max(qb):
                    dve.wait_ge(scores_done, sc.up())
                    s = aux[:, 1 + qb % 2, 0:qb * P + P]
                    link(dve.tensor_tensor(s[:, qb * P:], s[:, qb * P:], con("causal", P), ALU.add))
                    link(dve.tensor_reduce(small[:, qb:qb + 1], s, AX.X, ALU.max))
                    dve.tensor_scalar(small[:, 4 + qb:5 + qb], small[:, qb:qb + 1], -SCALE, None, ALU.mult).then_inc(bias_done, 1)
                    bs.up()

                def normal(qb):
                    at, n = qb * (qb + 1) // 2, qb + 1
                    dve.wait_ge(exp_done, en.up() + 2)
                    link(dve.reciprocal(small[:, 12 + qb:13 + qb], small[:, 8 + qb:9 + qb]))
                    dve.tensor_scalar(pr[:, at:at + n, :], pr[:, at:at + n, :], small[:, 12 + qb:13 + qb], None, ALU.mult).then_inc(probs_done, 1)

                def copy_turned(qb):
                    at, n = qb * (qb + 1) // 2, qb + 1
                    dve.wait_ge(turned, tn.up())
                    dve.tensor_copy(pt[:, at:at + n, :], aux[:, 3, 0:n * P].rearrange("p (b k) -> p b k", k=P)).then_inc(pt_done, 1)

                def first_blocks():
                    row_max(0)
                    row_max(1)
                    normal(0)
                    normal(1)

                def head(b, h, slot, nxt, z):
                    if nxt:
                        take_qn(1 - b)
                    copy_turned(0)
                    row_max(2)
                    if nxt:
                        take_qr(1 - b)
                    normal(2)
                    copy_turned(1)
                    row_max(3)
                    copy_turned(2)
                    normal(3)
                    if nxt:
                        take_kn(1 - b)
                        take_vt(1 - b)
                    if z is not None:
                        unit.up(2)
                        dve.wait_ge(slot_free, unit.now() + RING)
                        zt.up()
                        dve.tensor_tensor(zs[:, z, :], aux[:, 0, :], rstd[:, :], ALU.mult).then_inc(z_taken, 1)
                        if not nxt:
                            silus.up()
                    copy_turned(3)
                    if nxt:
                        first_blocks()
                    dve.wait_ge(silu_done, silus.now())
                    dve.wait_ge(heads_done, hd.up())
                    dve.tensor_tensor(og[:, h, :], aux[:, 0, :], zs[:, slot, :], ALU.mult).then_inc(og_done, 1)
                    dve.wait_ge(og_done, hd.now())
                    if z is not None and nxt:
                        silus.up()

                sc, bs, en, tn, hd, zt = (Count() for _ in range(6))
                silus.up(8)
                dve.memset(small[:, 0:1], 0.0).then_inc(exp_done, 2)
                dve.wait_ge(exp_done, 2)
                dve.memset(small[:, 0:1], 0.0).then_inc(pt_done, 1)
                dve.wait_ge(pt_done, 1)
                take_qn(0)
                take_qr(0)
                take_kn(0)
                take_vt(0)
                first_blocks()
                for first, pairs in ((0, 4), (4, 3)):
                    with Rolled(dve, pairs, {unit: 8, tile: 8, sc: 8, bs: 8, en: 8, tn: 8, hd: 2, zt: 1, silus: 1,
                                             step: 24}) as i:
                        head(0, i * 2 + 2 * first, i * 2, True, None)
                        head(1, i * 2 + (2 * first + 1), i * 2 + 1, True, i + first)
                head(0, IT - 2, 6, True, None)
                head(1, IT - 1, 7, False, 7)
                for k in range(IT):
                    als.up()
                    dve.wait_ge(ah_done, als.now())
                    dve.tensor_tensor(act_l[:, k, :], og[:, k, :], act_h[:, k, :].bitcast(F32),
                                      ALU.subtract).then_inc(al_done, 1)

            def hybrid_mixer():
                link(dve.memset(cpad[:, 0:3], 0.0))
                link(dve.memset(rows[:, :], 0.0))
                link(dve.memset(reset[:, :], 1.0))
                link(dve.memset(reset[:, 0::CHUNK], 0.0))

                def conv_tile(n, f):
                    take(dve.tensor_tensor(cpad[:, 3:3 + S], bank(2), rstd[:, :], ALU.mult))
                    if n >= 2:
                        dve.wait_ge(heads_in, 2 * n - 3 if n - 2 < 8 else 16 + n - 9)
                    y_ = cy[:, n % 2, :]
                    link(dve.tensor_scalar(y_, cpad[:, 0:S], par("dn_conv", f), None, ALU.mult))
                    for k in (1, 2, 3):
                        ins = dve.scalar_tensor_tensor(y_, cpad[:, k:k + S], par("dn_conv", f + 12 * k), y_, ALU.mult, ALU.add)
                        if k < 3:
                            link(ins)
                    ins.then_inc(conv_done, 1)
                    dve.wait_ge(conv_done, n + 1)

                for i in range(8):
                    conv_tile(i, (i + 4) % 8)
                take(dve.tensor_tensor(raw[:, :], bank(2), rstd[:, :], ALU.mult))
                for i in range(4):
                    conv_tile(8 + i, 8 + i)
                for to, scale in ((a_q[:, 0, :], 0.125), (a_q[:, 1, :], 0.125), (a_kv[:, 0, :], 1.0), (a_kv[:, 1, :], 1.0),
                                  (b_q[:, 0, :], 0.125), (b_q[:, 1, :], 0.125), (b_k[:, 0, :], 1.0), (b_k[:, 1, :], 1.0),
                                  (b_v[:, 0, :], 1.0), (b_v[:, 1, :], 1.0)):
                    take(dve.scalar_tensor_tensor(to, bank(2), scale, rstd[:, :], ALU.mult, ALU.mult))
                for i in range(4):
                    take(dve.tensor_tensor(zc[:, i, :], bank(2), rstd[:, :], ALU.mult))

                def made(ins, name):
                    ins.then_inc(mix_dve, 1)
                    dve.wait_ge(mix_dve, DVE_STEP.next(name))

                dve.wait_ge(heads_in, 24)
                link(dve.tensor_scalar(raw[32:36, :], raw[32:36, :],
                                       params[32:36, PARAMS["dt_bias"]:PARAMS["dt_bias"] + 1], None, ALU.add))
                made(dve.scalar_tensor_tensor(absy[32:36, :], raw[32:36, :], -1.0, raw[32:36, :], ALU.mult, ALU.max), "ydt")
                dve.wait_ge(mix_act, ACT_STEP["nega"])
                made(dve.tensor_scalar(rows[0:4, :], raw[0:4, :], 0.5, 0.5, ALU.mult, ALU.add), "beta")
                link(dve.scalar_tensor_tensor(raw[32:36, :], raw[32:36, :], 0.0, absy[32:36, :], ALU.max, ALU.add))
                link(dve.tensor_scalar(raw[32:36, :], raw[32:36, :], nega[32:36, :], -1.0, ALU.mult, ALU.mult))
                link(dve.tensor_tensor_scan(rows[32:36, :], reset[32:36, :], raw[32:36, :], 0.0, ALU.mult, ALU.add))
                made(dve.tensor_copy(rows[64:68, :].rearrange("p (c k) -> p c k", k=CHUNK),
                                     rows[32:36, CHUNK - 1::CHUNK].unsqueeze(2).broadcast_to([4, 8, CHUNK])), "g")
                dve.wait_ge(mix_act, ACT_STEP["sqrt"])
                made(dve.reciprocal(rc[:, :], rc[:, :]), "rc")
                dve.wait_ge(mix_pe, PE_STEP["rnt"])
                made(dve.tensor_copy(rn[0:8, :], banks(1)[0:8, :]), "rn")
                dve.wait_ge(mix_pe, PE_STEP["rowt"])
                made(dve.tensor_copy(cols[:, :, :], banks(2)[:, 0:4 * 68].rearrange("p (b k) -> p b k", k=68)), "cols")
                dve.wait_ge(mix_act, ACT_STEP["cexp"])
                link(dve.tensor_tensor(cbe[:, :, :], cols[:, :, 0:4], ceg[:, :, :], ALU.mult))
                made(dve.tensor_tensor(ckd[:, :, :], cols[:, :, 64:68], cols[:, :, 32:36], ALU.subtract), "cd")
                dve.wait_ge(consts2_loaded, 16)
                mask_t = consts2[:, CONSTS2["mask_t"]:CONSTS2["mask_t"] + P]
                heads = range(4)
                for h in heads:
                    dve.wait_ge(mix_pe, PE_STEP["bk", h])
                    made(dve.tensor_tensor(kf[:, h, :], kf[:, h, :], head_bank(h, 0), ALU.mult), ("kf", h))
                for h in heads:
                    dve.wait_ge(mix_pe, PE_STEP["bq", h])
                    made(dve.scalar_tensor_tensor(qf[:, h, :], head_bank(h, 1), P ** -0.5, qf[:, h, :],
                                                  ALU.mult, ALU.mult), ("qf", h))
                for h in heads:
                    dve.wait_ge(mix_pe, PE_STEP["bb", h])
                    made(dve.tensor_tensor(e_mat[:, h, :, :], blocks_of(kf[:, h, :]), blocks_of(head_bank(h, 0)),
                                           ALU.mult), ("kb", h))
                for h in heads:
                    dve.wait_ge(mix_pe, PE_STEP["bg", h])
                    for blk in range(4):
                        ins = dve.scalar_tensor_tensor(d_mat[:, h, blk, :], head_bank(h, 1)[:, blk * P:blk * P + P],
                                                       cols[:, blk, 32 + h:33 + h], mask_t, ALU.subtract, ALU.add)
                    made(ins, ("dt", h))
                for h in heads:
                    dve.wait_ge(mix_pe, PE_STEP["kt", h])
                    for blk in range(4):
                        if h == 0 and blk == 0:
                            dve.wait_ge(mix_pe, PE_STEP["vt", 3])
                            dve.wait_ge(mix_act, ACT_STEP["ckd"])
                        ins = dve.tensor_scalar(vf[:, h, blk * P:blk * P + P], head_bank(h, 0)[:, blk * P:blk * P + P],
                                                cbe[:, blk, h:h + 1], None, ALU.mult)
                    made(ins, ("kbe", h))
                    for blk in range(4):
                        ins = dve.tensor_scalar(kdec[:, h, blk, :], head_bank(h, 0)[:, blk * P:blk * P + P],
                                                ckd[:, blk, h:h + 1], None, ALU.mult)
                    made(ins, ("kd", h))
                for h in heads:
                    dve.wait_ge(mix_pe, PE_STEP["g1", h])
                    dve.wait_ge(mix_act, ACT_STEP["edt", h])
                    made(dve.tensor_tensor(l_mat[:, h, :, :], blocks_of(head_bank(h, 0)), d_mat[:, h, :, :],
                                           ALU.mult), ("lt", h))
                    link(dve.tensor_tensor(xt[:, h, :, :], l_mat[:, h, :, :], level(0), ALU.mult))
                    made(dve.scalar_tensor_tensor(xt[:, h, :, :], xt[:, h, :, :], -1.0,
                                                  con("ident", P).unsqueeze(1).broadcast_to([P, 4, P]),
                                                  ALU.mult, ALU.add), ("xt0", h))
                    made(dve.tensor_tensor(e_mat[:, h, :, :], l_mat[:, h, :, :], level(1), ALU.mult), ("e1", h))
                for h in heads:
                    dve.wait_ge(mix_pe, PE_STEP["g2", h])
                    made(dve.tensor_tensor(blocks_of(kf[:, h, :]), blocks_of(head_bank(h, 1)), d_mat[:, h, :, :],
                                           ALU.mult), ("at", h))
                    made(dve.tensor_tensor(qf[:, h, :], qf[:, h, :], eg[:, h, :, :].rearrange("p b k -> p (b k)"),
                                           ALU.mult), ("qd", h))
                for l in range(1, LEVELS):
                    if l < LEVELS - 1:
                        for h in heads:
                            dve.wait_ge(mix_pe, PE_STEP[f"y{l}", h])
                            made(dve.tensor_tensor(e_mat[:, h, :, :], l_mat[:, h, :, :], level(l + 1), ALU.mult), (f"e{l + 1}", h))
                    for h in heads:
                        dve.wait_ge(mix_pe, PE_STEP[f"p{l}", h])
                        if l < LEVELS - 1:
                            link(dve.tensor_tensor(x_mat[:, h, :, :], x_mat[:, h, :, :], blocks_of(head_bank(h, 1)),
                                                   ALU.subtract))
                        made(dve.tensor_tensor(xt[:, h, :, :], xt[:, h, :, :], blocks_of(head_bank(h, 0)),
                                               ALU.subtract), (f"xt{l}", h))

                def attend(slot):
                    n = slot
                    if n < 32:
                        tl, qb, half, first, w = attention_block(n)
                        s = score_rows[n % 3][:, 0:w]
                        if tl < 2:
                            at, slope = CONSTS2["dist_swa"] + 2 * P - w, SLOPES_SWA[2 * tl + half]
                        else:
                            at, slope = CONSTS2["dist"] + 4 * P - w, SLOPES_MOBA[2 * (tl - 2) + half]
                        dve.wait_ge(mix_pe, PE_STEP["s", n])
                        link(dve.scalar_tensor_tensor(s, consts2[:, at:at + w], -slope, banks(3 + n % 2)[:, 0:w],
                                                      ALU.mult, ALU.add))
                        top = soft[:, n % 3, 0:1]
                        link(dve.tensor_reduce(top, s, AX.X, ALU.max))
                        if tl < 2:
                            head = PARAMS["sinks"] + 2 * tl + half
                            made(dve.tensor_scalar(top, top, params[:, head:head + 1], -1.0, ALU.max, ALU.mult), ("mx", n))
                        else:
                            made(dve.tensor_scalar(top, top, -1.0, None, ALU.mult), ("mx", n))
                    n = slot - 1
                    if 0 <= n < 32:
                        tl, qb, half, first, w = attention_block(n)
                        s, k = score_rows[n % 3][:, 0:w], n % 3
                        dve.wait_ge(mix_act, ACT_STEP["ex", n])
                        if tl < 2:
                            link(dve.tensor_tensor(soft[:, k, 1:2], soft[:, k, 1:2], soft[:, k, 2:3], ALU.add))
                        link(dve.reciprocal(soft[:, k, 3:4], soft[:, k, 1:2]))
                        made(dve.tensor_scalar(s, s, soft[:, k, 3:4], None, ALU.mult), ("nr", n))

                slot = 0
                for c in range(8):
                    if c < 7:
                        dve.wait_ge(mix_pe, PE_STEP["su", c])
                        for h in range(4):
                            if c:
                                ins = dve.scalar_tensor_tensor(state[:, h, :], state[:, h, :], egl[:, h, c:c + 1],
                                                               banks(1)[:, h * P:h * P + P], ALU.mult, ALU.add)
                            else:
                                ins = dve.tensor_copy(state[:, h, :], banks(1)[:, h * P:h * P + P])
                        made(ins, ("st", c))
                    for _ in range(4 if c < 7 else 7):
                        attend(slot)
                        slot += 1
                dve.wait_ge(mix_act, ACT_STEP["osqrt"])
                made(dve.reciprocal(rc[:, 0:16], rc[:, 0:16]), "orc")
                dve.wait_ge(mix_pe, PE_STEP["ornt"])
                made(dve.tensor_copy(rn[0:4, :], banks(1)[0:4, :]), "orn")
                for h in range(4):
                    dve.wait_ge(mix_pe, PE_STEP["ob", h])
                    link(dve.scalar_tensor_tensor(mixed[:, 4 + h, :], mixed[:, 4 + h, :], par("dn_norm", 0), banks(2 + h % 2),
                                                  ALU.mult, ALU.mult))
                    made(dve.tensor_tensor(mixed[:, 4 + h, :], mixed[:, 4 + h, :], zc[:, h, :], ALU.mult), ("on", h))
                for k in range(DT):
                    als.up()
                    dve.wait_ge(ah_done, als.now())
                    dve.tensor_tensor(act_l[:, k, :], mixed[:, k, :], act_h[:, k, :].bitcast(F32),
                                      ALU.subtract).then_inc(al_done, 1)

            dve.memset(ssum[:, :], 0.0).then_inc(taken, BANKS)
            dve.memset(std[:, :], 0.0).then_inc(slot_free, RING)
            dve.wait_ge(taken, BANKS)
            dve.wait_ge(slot_free, RING)
            dve.memset(rstd[:, :], 0.0).then_inc(ready, 1)
            dve.wait_ge(ready, 1)
            for f in range(DT):
                residual_tile(f, phases[0] != "final" and NORM_OF[phases[0]])
            deviation()
            for n, ph in enumerate(phases):
                nxt = NORM_OF[phases[n + 1]] if split_after(n) else None
                if ph.startswith("pool"):
                    link(dve.memset(upad[:, :, 0:PAD], 0.0))
                    for g, w in enumerate(WINDOWS):
                        for t in range(4):
                            u = upad[:, t % 2, :]
                            take(dve.tensor_tensor(u[:, PAD:PAD + S], bank(2), rstd[:, :], ALU.mult))
                            link(dve.tensor_tensor_scan(wsum[:, :], u[:, PAD:PAD + S], u[:, PAD - w:PAD - w + S],
                                                        0.0, ALU.add, ALU.subtract))
                            link(dve.tensor_tensor(wsum[:, 0:PAD], wsum[:, 0:PAD], con("poolfix", PAD, PAD * g),
                                                   ALU.mult))
                            dve.scalar_tensor_tensor(prod[:, :], wsum[:, :], 1.0 / w, u[:, PAD:PAD + S],
                                                     ALU.mult, ALU.subtract).then_inc(prod_done, 1)
                            dve.wait_ge(prod_done, prods.up())
                            rest(4 + 4 * g + t)
                    with Rolled(dve, 4, {unit: 12, tile: 8, silus: 4, als: 4}) as g:
                        for t in range(4):
                            take(dve.tensor_tensor(z4[:, t, :], bank(2), rstd[:, :], ALU.mult))
                        for t in range(4):
                            b = bank(1)
                            dve.wait_ge(silu_done, silus.up())
                            take(dve.scalar_tensor_tensor(prod[:, :], b, par("pool_scale" + ph[-1], g * 4 + t),
                                                          z4[:, t, :], ALU.mult, ALU.mult))
                            rest(g * 4 + t)
                    out_tiles(4, nxt)
                if ph == "conv":
                    link(dve.memset(qpad[:, 0:2], 0.0))
                    with Rolled(dve, IT, {unit: 8, tile: 4, silus: 1, als: 1, prods: 1, step: 5}) as f:
                        take(dve.tensor_tensor(cb[:, :], bank(2), rstd[:, :], ALU.mult))
                        take(dve.tensor_tensor(hb[:, :], bank(2), rstd[:, :], ALU.mult))
                        link(dve.tensor_tensor(qpad[:, 2:2 + S], cb[:, :], hb[:, :], ALU.mult))
                        link(dve.tensor_scalar(yb[:, :], qpad[:, 0:S], par("conv_w", f), None, ALU.mult))
                        for k in (1, 2):
                            link(dve.scalar_tensor_tensor(yb[:, :], qpad[:, k:k + S], par("conv_w", f + IT * k),
                                                          yb[:, :], ALU.mult, ALU.add))
                        take(dve.tensor_tensor(hb[:, :], bank(2), rstd[:, :], ALU.mult))
                        link(dve.tensor_tensor(yb[:, :], yb[:, :], hb[:, :], ALU.mult))
                        take(dve.tensor_tensor(zb[:, :], bank(2), rstd[:, :], ALU.mult))
                        dve.wait_ge(silu_done, silus.up())
                        dve.tensor_tensor(prod[:, :], yb[:, :], zb[:, :], ALU.mult).then_inc(prod_done, 1)
                        dve.wait_ge(prod_done, prods.up())
                        rest(f)
                    out_tiles(4, nxt)
                if ph == "mla":
                    latent_attention()
                    out_tiles(4, nxt)
                if ph == "final":
                    for f in range(DT):
                        dve.scalar_tensor_tensor(x[:, f, :], x[:, f, :], par("final_norm", f), rstd[:, :],
                                                 ALU.mult, ALU.mult).then_inc(x_done, 1)
                        dve.wait_ge(x_done, xs.up())
                        if f:
                            residual_tile(f - 1, nxt)
                    residual_tile(DT - 1, nxt)
                    deviation()
                if ph == "mixer":
                    hybrid_mixer()
                    out_tiles(2, None, of=y)
                    add_normed("mix_post", nxt)
                if ph == "ffn":
                    link(dve.memset(gpad[:, :, 0:2], 0.0))

                    def conv3(t, f, n):
                        take(dve.tensor_tensor(gpad[:, t, 2:2 + S], bank(2), rstd[:, :], ALU.mult))
                        link(dve.tensor_scalar(yg[:, t, :], gpad[:, t, 0:S], par("ffn_conv_w", f),
                                               par("ffn_conv_b", f), ALU.mult, ALU.add))
                        link(dve.scalar_tensor_tensor(yg[:, t, :], gpad[:, t, 1:1 + S], par("ffn_conv_w", f + 2 * FT),
                                                      yg[:, t, :], ALU.mult, ALU.add))
                        return dve.scalar_tensor_tensor(yg[:, t, :], gpad[:, t, 2:2 + S],
                                                        par("ffn_conv_w", f + 4 * FT), yg[:, t, :], ALU.mult, ALU.add)

                    with Rolled(dve, FT // 2, {unit: 8, tile: 4, gates: 2, silus: 2, prods: 2, als: 2, step: 10}) as i:
                        for t in range(2):
                            f = i * 2 + t
                            conv3(0, f, t).then_inc(gate_done, 1)
                            gates.up()
                            link(conv3(1, f + FT, t))
                            dve.wait_ge(silu_done, silus.up())
                            dve.tensor_tensor(prod[:, :], yg[:, 0, :], yg[:, 1, :], ALU.mult).then_inc(prod_done, 1)
                            dve.wait_ge(prod_done, prods.up())
                            rest(f)
                    out_tiles(6, None, of=y)
                    add_normed("ffn_post", None)
            if phases[-1] != "ffn":
                dve.memset(ssum[:, :], 0.0).then_inc(x_done, 1)


NORM_OF = {"pool0": "pool_norm0", "pool1": "pool_norm1", "conv": "conv_norm", "mla": "mla_norm",
           "final": "final_norm", "mixer": "mix_pre", "ffn": "ffn_pre"}


def weight_blocks(a, phase):
    import numpy as np

    out = []

    def tile(w, cols, pad=None):
        ks = w.shape[0] // P
        for k in range(ks):
            out.append(w[k * P:(k + 1) * P, cols:cols + P])
        for _ in range((-ks) % 4 if pad is None else pad):
            out.append(np.zeros((P, P), np.float32))

    if phase.startswith("pool"):
        j = int(phase[-1])
        w_in, w_grp, w_out = a["pool_w_in"][j], a["pool_w_grp"][j], a["pool_w_out"][j]
        for f in range(IT):
            tile(w_in, f * P)
        for g in range(4):
            for t in range(4):
                tile(w_in, DI + (4 * g + t) * P)
            for t in range(4):
                tile(w_grp[g], t * P)
        for f in range(DT):
            tile(w_out, f * P)
    if phase == "conv":
        w_in = a["conv_w_in"][0]
        for f in range(IT):
            for part in (1, 2, 0, 3):
                tile(w_in, part * DI + f * P)
        for f in range(DT):
            tile(a["conv_w_out"][0], f * P)
    if phase == "mla":
        w_in, q_up, kv_up = a["mla_w_in"][0], a["mla_w_q_up"][0], a["mla_w_kv_up"][0]
        rope = w_in[:, 640:704]
        z_in = w_in[:, 704:]

        def with_halves_swapped(w):
            return np.concatenate([w, w[:, 32:], w[:, :32]], axis=1)

        def q_head(h):
            w = q_up[:, 192 * h:192 * h + 192]
            tile(w[:, :P], 0)
            tile(with_halves_swapped(w[:, P:]), 0)

        def kv_head(h):
            tile(kv_up, 256 * h, pad=0)
            tile(kv_up, 256 * h + P, pad=0)

        for f in range(5):
            tile(w_in, f * P)
        tile(with_halves_swapped(rope), 0)
        for f in range(8):
            tile(z_in, f * P)
        q_head(0)
        kv_head(0)
        for h in range(16):
            if h < 15:
                q_head(h + 1)
                kv_head(h + 1)
            if h % 2:
                tile(z_in, (8 + h // 2) * P)
        for f in range(DT):
            tile(a["mla_w_out"][0], f * P)
    if phase == "mixer":
        w = a["w_in_2"][0]
        q_a, k_a, v_a, q_b, k_b, v_b, qkv_c, z_c, b_c, a_c = np.split(
            w, np.cumsum([256, 128, 128, 256, 256, 256, 1536, 512, 4]), axis=1)
        for f in (4, 5, 6, 7, 0, 1, 2, 3):
            tile(qkv_c, f * P)
        ba = np.zeros((D, P), np.float32)
        ba[:, 0:4], ba[:, 32:36] = b_c, a_c
        tile(ba, 0)
        for f in range(8, 12):
            tile(qkv_c, f * P)
        tile(np.concatenate([q_a[:, 0:64], q_a[:, 128:192]], axis=1), 0)
        tile(np.concatenate([q_a[:, 64:128], q_a[:, 192:256]], axis=1), 0)
        tile(k_a, 0)
        tile(v_a, 0)
        for m in (q_b, k_b, v_b):
            tile(m, 0)
            tile(m, P)
        for f in range(4):
            tile(z_c, f * P)
        for f in range(DT):
            tile(a["w_out_2"][0], f * P)
    if phase == "ffn":
        for f in range(FT):
            tile(a["w_up_2"][0], f * P)
            tile(a["w_up_2"][0], FF + f * P)
        for f in range(DT):
            tile(a["w_down_2"][0], f * P)
    return out


def pack(a, phases):
    import numpy as np

    blocks = [b for ph in phases for b in weight_blocks(a, ph)]
    blocks += [np.zeros((P, P), np.float32)] * (4 * n_units(phases) - len(blocks))
    w = np.stack(blocks).reshape(-1, 8, P, P)
    stream = np.ascontiguousarray(w.transpose(0, 2, 1, 3)).reshape(-1, P, 8 * P)

    params = np.zeros((P, NPARAMS), np.float32)

    def put(name, v, at=0):
        v = np.asarray(v).reshape(-1, P).T
        params[:, PARAMS[name] + at:PARAMS[name] + at + v.shape[1]] = v

    put("pool_norm0", a["pool_norm"][0]); put("pool_norm1", a["pool_norm"][1])
    put("conv_norm", a["conv_norm"][0]); put("mla_norm", a["mla_norm"][0]); put("final_norm", a["final_norm"])
    put("mix_pre", a["mix_pre_norm_2"][0]); put("mix_post", a["mix_post_norm_2"][0])
    put("ffn_pre", a["ffn_pre_norm_2"][0]); put("ffn_post", a["ffn_post_norm_2"][0])
    put("pool_scale0", a["pool_scale"][0]); put("pool_scale1", a["pool_scale"][1])
    put("conv_w", a["conv_w"][0]); put("q_norm", a["mla_q_norm"][0]); put("kv_norm", a["mla_kv_norm"][0])
    put("ffn_conv_w", a["ffn_conv_w_2"][0]); put("ffn_conv_b", a["ffn_conv_b_2"][0])
    put("dn_conv", a["dn_conv_w_2"][0]); put("dn_norm", a["dn_norm_2"][0])
    params[:, PARAMS["sinks"]:PARAMS["sinks"] + 4] = a["swa_sinks_2"][0][None, :]
    params[32:36, PARAMS["a_log"]] = a["dn_a_log_2"][0]
    params[32:36, PARAMS["dt_bias"]] = a["dn_dt_bias_2"][0]

    consts = np.zeros((P, NCONSTS), np.float32)
    p, c = np.arange(P)[:, None], np.arange(P)[None, :]
    consts[:, CONSTS["ident"]:CONSTS["ident"] + P] = p == c
    consts[:, CONSTS["fold"]:CONSTS["fold"] + P] = p % 64 == c % 64
    consts[:, CONSTS["causal"]:CONSTS["causal"] + P] = np.where(c <= p, 0.0, -1e30)
    for g, w in enumerate(WINDOWS):
        t = np.arange(PAD)
        consts[:, CONSTS["poolfix"] + g * PAD:CONSTS["poolfix"] + (g + 1) * PAD] = w / np.minimum(t + 1, w)
    i = np.arange(P)
    inv = 10000.0 ** (-2.0 * (i % 32) / 64)
    inv = inv.astype(np.float32)
    consts[:, CONSTS["freq"]] = np.where((i >= 64) & (i < 96), -inv, inv)
    consts[:, CONSTS["phase"]] = np.where(i < 64, np.float32(np.pi / 2), 0.0)
    consts[:, CONSTS["eps"]] = EPS
    c2 = np.zeros((P, NCONSTS2), np.float32)
    for l in range(LEVELS):
        s = 1 << l
        c2[:, l * P:l * P + P] = (p // (2 * s) == c // (2 * s)) & (p // s % 2 == 0) & (c // s % 2 == 1)
    c2[:, CONSTS2["mask_t"]:CONSTS2["mask_t"] + P] = np.where((p // CHUNK == c // CHUNK) & (c >= p), 0.0, -1e30)
    k = np.arange(4 * P)[None, :]
    c2[:, CONSTS2["dist"]:CONSTS2["dist"] + 4 * P] = np.where(p + 3 * P >= k, p + 3 * P - k, FAR)
    rel = p + P - k[:, :2 * P]
    c2[:, CONSTS2["dist_swa"]:CONSTS2["dist_swa"] + 2 * P] = np.where((rel >= 0) & (rel < P), rel, FAR)
    return {
        "consts2": c2,
        "x": np.ascontiguousarray(a["x"].reshape(S, DT, P).transpose(2, 1, 0)),
        "stream": stream, "params": params, "consts": consts,
        "pos": np.ascontiguousarray(np.broadcast_to(a["positions"].reshape(1, S), (P, S))),
    }


def kernel(**inputs):
    import numpy as np
    import concourse.bacc as bacc
    from concourse import mybir as mb
    from concourse.bass_utils import run_bass_kernel_spmd

    a = {k: np.asarray(v) for k, v in inputs.items()}
    arrays = pack(a, PHASES)
    nc = bacc.Bacc("TRN2", target_bir_lowering=False, num_devices=1)
    aps = {n: nc.dram_tensor(n, v.shape, mb.dt.from_np(v.dtype), kind="ExternalInput").ap() for n, v in arrays.items()}
    out = nc.dram_tensor("out", (P, DT, S), F32, kind="ExternalOutput").ap()
    program(nc, aps["x"], aps["stream"], aps["params"], aps["consts"], aps["consts2"], aps["pos"], out, PHASES)
    r = run_bass_kernel_spmd(nc, [arrays], core_ids=[0])
    return np.ascontiguousarray(r.results[0]["out"].transpose(2, 1, 0)).reshape(1, S, D)
```

```python
import concourse.bass as bass
import concourse.mybir as mybir
from contextlib import ExitStack

F32 = mybir.dt.float32
F32R = mybir.dt.float32r
I32 = mybir.dt.int32
ALU = mybir.AluOpType
ACT = mybir.ActivationFunctionType
AX = mybir.AxisListType

P = 128
S = 512
D = 1024
DI = 2048
DT = D // P
IT = DI // P
FF = 2816
FT = FF // P
WINDOWS = (2, 4, 8, 16)
PAD = 16
CONV = 3
SCALE = (128 + 64) ** -0.5
EPS = 1e-6
TWO_PI = 6.283185307179586
TWO_PI_PARTS = (6.28125, 0.0019350051879882812, 3.0199159795074593e-07)
TOGETHER = 3
GROUPED = ("mixer", "ffn")
FIRST_HIS = (2, 2, 2, 2, 1, 1, 1, 1)
LEVELS = 6
CHUNK = 64
SLOPES = [2.0 ** -(i + 1) for i in range(8)]
SLOPES_SWA, SLOPES_MOBA = SLOPES[0::2], SLOPES[1::2]
FAR = 1e32
RING = 4
BANKS = 4
PHASES = ("pool0", "conv", "mla", "pool1", "final", "mixer", "ffn")

PARAMS = {}
_at = 0
for _name, _n in (("pool_norm0", DT), ("pool_norm1", DT), ("conv_norm", DT), ("mla_norm", DT), ("final_norm", DT),
                  ("mix_pre", DT), ("mix_post", DT), ("ffn_pre", DT), ("ffn_post", DT),
                  ("pool_scale0", IT), ("pool_scale1", IT), ("conv_w", CONV * IT), ("q_norm", 3), ("kv_norm", 2),
                  ("ffn_conv_w", CONV * 2 * FT), ("ffn_conv_b", 2 * FT), ("dn_conv", 4 * 12), ("dn_norm", 1),
                  ("sinks", 4), ("a_log", 1), ("dt_bias", 1)):
    PARAMS[_name] = _at
    _at += _n
NPARAMS = _at
CONSTS = {}
_at = 0
for _name, _n in (("ident", P), ("fold", P), ("causal", P), ("poolfix", 4 * PAD), ("freq", 1), ("phase", 1),
                  ("eps", 1)):
    CONSTS[_name] = _at
    _at += _n
NCONSTS = _at


CONSTS2 = {}
_at = 0
for _name, _n in (("levels", LEVELS * P), ("mask_t", P), ("dist", 4 * P), ("dist_swa", 2 * P)):
    CONSTS2[_name] = _at
    _at += _n
NCONSTS2 = _at


class Count:

    def __init__(self, start=0):
        self.n, self.i, self.per = start, None, 0

    def up(self, by=1):
        self.n += by
        return self.now()

    def now(self, ahead=0):
        return self.n + ahead if self.i is None else self.i * self.per + (self.n + ahead)

    def enter(self, i, per):
        self.i, self.per, self.first = i, per, self.n

    def leave(self, times):
        assert self.n == self.first + self.per, (self.n, self.first, self.per)
        self.n, self.i = self.first + self.per * times, None


class Steps:

    def __init__(self, names):
        self.names, self.value = names, {name: n + 1 for n, name in enumerate(names)}
        assert len(self.value) == len(names)
        self.made = 0

    def next(self, name):
        assert self.names[self.made] == name, (self.names[self.made], name)
        self.made += 1
        return self.made

    def __getitem__(self, name):
        return self.value[name]


HEADS = range(4)
CHUNKS = S // CHUNK
PAIRS = 16


def mixer_steps():
    def each(*names):
        return [(n, h) for h in HEADS for n in names]

    pe = each("ssk") + each("ssq") + ["rowt"] + each("bb") + each("bg") + each("vt") + each("kt") + each("g1") + each("g2")
    pe += each("x1") + each("bg2")
    dve = ["ydt", ("kf", 0), ("kf", 1), "beta", "g", ("kf", 2), ("kf", 3), "cols", ("qf", 0), "cd"] + each("kb")
    dve += [("qf", 1)] + each("dt") + [("qf", 2), ("qf", 3)] + each("kbe") + each("lt", "xt0") + each("at")
    dve += each("e1") + each("qd")
    act = ["tanh", "e1", "ln", "nega"] + each("sk") + each("sq") + each("zs") + ["cexp", "ckd"] + each("egl", "edt")
    act += each("vb") + each("kd") + each("xc") + each("eg")
    for l in range(1, LEVELS):
        pe += each(f"y{l}") + each(f"p{l}")
        dve += (each(f"e{l + 1}") if l < LEVELS - 1 else []) + each(f"xt{l}")
        act += each(f"yc{l}")
    pe += each("wt")
    act += each("nw")
    dve += ["slopes"]
    for blk in range(4):
        pe += [("av", blk)]
        act += [("avc", blk)]

    def attend(k):
        if 1 <= k <= PAIRS:
            dve.append(("nr", k - 1))
        if k < PAIRS:
            pe.append(("s", k))
            dve.append(("mx", k))
            act.append(("ex", k))

    def turn(k):
        if 1 <= k <= PAIRS:
            pe.append(("t", k - 1))
            act.append(("pc", k - 1))

    def values(k):
        if 2 <= k:
            pe.append(("pv", k - 2))
            act.append(("mc", k - 2))

    for c in range(CHUNKS):
        act += [("vn", c)]
        attend(2 * c)
        pe += [("nv", c)]
        turn(2 * c)
        pe += [("o", c)] + ([("su", c)] if c < CHUNKS - 1 else [])
        act += [("oc", c)]
        dve += [("st", c)] if c < CHUNKS - 1 else []
        if c % 2:
            act += [("osq", c // 2)]
        values(2 * c)
        attend(2 * c + 1)
        turn(2 * c + 1)
        if c % 2:
            pe += [("osum", c // 2)]
        values(2 * c + 1)
    for k in (PAIRS, PAIRS + 1):
        attend(k)
        turn(k)
        values(k)
    pe += ["ornt"] + each("ob")
    act += ["osqrt"]
    dve += ["orc", "orn"] + each("on")
    return pe, dve, act


class Rolled:

    def __init__(self, eng, times, pers):
        self.times, self.pers, self.loop = times, pers, eng.Fori(0, times)

    def __enter__(self):
        i = self.loop.__enter__()
        for c, per in self.pers.items():
            c.enter(i, per)
        return i

    def __exit__(self, *a):
        self.loop.__exit__(*a)
        if a[0] is None:
            for c in self.pers:
                c.leave(self.times)


def x_updates(phases):
    return sum(p in ("final", "mixer", "ffn") for p in phases)


def n_units(phases):
    per = {"pool0": 2 * IT + 2 * IT + IT + 4 * DT, "conv": 8 * IT + 4 * DT, "mla": 28 + 16 * 3 + 16 + 4 * DT,
           "final": 0, "mixer": 2 * 27 + 2 * DT, "ffn": 2 * 2 * FT + 6 * DT}
    per["pool1"] = per["pool0"]
    return sum(per[p] for p in phases) + RING


def program(nc, x_in, stream, params_in, consts_in, consts2_in, pos_in, out, phases):
    ctx = ExitStack()
    with ctx:
        def sb(name, shape, dt=F32, on=ctx):
            return on.enter_context(nc.sbuf_tensor(name, shape, dt))

        def sem(name):
            return ctx.enter_context(nc.semaphore(name))

        x = sb("x_res", [P, DT, S])
        late = ExitStack()
        x_mat = sb("x_mat", [P, 4, 4, P], F32, late)
        y_mat = sb("y_mat", [P, 4, 4, P], F32, late)
        e_mat = sb("e_mat", [P, 4, 4, P], F32, late)
        v_tok = sb("v_tok", [P, 4, 3, P], F32, late)
        eg = y_mat
        late.close()
        late = ExitStack()
        probs = sb("probs", [P, 2, 2, S], F32, late)
        slope_ident = sb("slope_ident", [P, 8, P], F32, late)
        osq = sb("osq", [P, 2, 4, P], F32, late)
        probs_t = sb("probs_t", [P, 2, 2, S], F32, late)
        late.close()
        xh = sb("xh", [P, DT, S], F32R)
        xl = sb("xl", [P, DT, S], F32R)
        w_stage = sb("w_stage", [P, RING, S])
        w_hi = sb("w_hi", [P, RING, S], F32R)
        w_lo = sb("w_lo", [P, RING, S], F32R)
        params = sb("params_sb", [P, NPARAMS])
        consts = sb("consts_sb", [P, NCONSTS])
        ones = sb("ones", [P, P])
        rstd = sb("rstd", [P, S])
        std = sb("std", [P, S])
        sq = sb("sq", [P, 2, S])
        ssum = sb("ssum", [P, S])
        cs = sb("cs", [P, S])
        small = sb("small", [P, 16])
        prod = sb("prod", [P, S])
        spare = ExitStack()
        act_l = sb("act_l", [P, FT, S], F32R, spare)
        act_h = sb("act_h", [P, FT, S], F32R, spare)
        zone = ExitStack()
        upad = sb("upad", [P, 2, PAD + S], F32, zone)
        wsum = sb("wsum", [P, S], F32, zone)
        z4 = sb("z4", [P, 4, S], F32, zone)
        zone.close()
        zone = ExitStack()
        cb = sb("cb", [P, S], F32, zone)
        hb = sb("hb", [P, S], F32, zone)
        qpad = sb("qpad", [P, 2 + S], F32, zone)
        yb = sb("yb", [P, S], F32, zone)
        zb = sb("zb", [P, S], F32, zone)
        zone.close()
        zone = ExitStack()
        gpad = sb("gpad", [P, 2, 2 + S], F32, zone)
        yg = sb("yg", [P, 2, S], F32, zone)
        y = sb("y", [P, DT, S], F32, zone)
        zone.close()
        spare.close()

        over = ExitStack()
        og = sb("og", [P, IT, S], F32, over)
        lat = sb("lat", [P, 5, S], F32, over)
        lat_h = sb("lat_h", [P, 5, S], F32R, over)
        lat_l = sb("lat_l", [P, 5, S], F32R, over)
        rlat = sb("rlat", [P, S], F32, over)
        sum_kv = sb("sum_kv", [P, S], F32, over)
        k_rot = sb("k_rot", [P, S], F32, over)
        tk = sb("tk", [P, S], F32, over)
        qn = sb("qn", [P, 2, S], F32, over)
        qr = sb("qr", [P, 2, S], F32, over)
        kn = sb("kn", [P, 2, S], F32, over)
        vt = sb("vt", [P, 2, S], F32, over)
        pr = sb("pr", [P, 10, P], F32, over)
        pt = sb("pt", [P, 10, P], F32, over)
        zs = sb("zs", [P, 8, S], F32, over)
        over.close()
        over = ExitStack()
        pos_i = sb("pos_i", [P, S], I32, over)
        turns_i = sb("turns_i", [P, S], I32, over)
        turns = sb("turns", [P, S], F32, over)
        angle = sb("angle", [P, S], F32, over)
        over.close()

        over = ExitStack()
        mixed = sb("mixed", [P, DT, S], F32, over)
        consts2 = sb("consts2_sb", [P, NCONSTS2], F32, over)
        kb, decay = mixed[:, 0:4, :], mixed[:, 4:8, :]
        l_mat = kb.rearrange("p h (b k) -> p h b k", k=P)
        zc = sb("zc", [P, 4, S], F32, over)
        qf = sb("qf", [P, 4, S], F32, over)
        a_q = sb("a_q", [P, 2, S], F32, over)
        raw = sb("raw", [P, S], F32, over)
        kf = sb("kf", [P, 4, S], F32, over)
        vf = sb("vf", [P, 4, S], F32, over)
        cpad = sb("cpad", [P, 4 + S], F32, over)
        rows = sb("rows", [P, S], F32, over)
        a_kv = sb("a_kv", [P, 2, S], F32, over)
        b_q = sb("b_q", [P, 2, S], F32, over)
        b_k = sb("b_k", [P, 2, S], F32, over)
        b_v = sb("b_v", [P, 2, S], F32, over)
        xt = sb("xt", [P, 4, 4, P], F32, over)
        squares_over = ExitStack()
        squares8 = sb("squares8", [P, 8, S], F32, squares_over)
        squares_over.close()
        vbeta = sb("vbeta", [P, 4, 4, P], F32, over)
        kdec = sb("kdec", [P, 4, 4, P], F32, over)
        reset = sb("reset", [P, S], F32, over)
        state = sb("state", [P, 4, P], F32, over)
        vnew = sb("vnew", [P, S], F32, over)
        cy = sb("cy", [P, 2, S], F32, over)
        cols = sb("cols", [P, 4, 68], F32, over)
        rc = sb("rc", [P, 16], F32, over)
        ceg = sb("ceg", [P, 4, 4], F32, over)
        cbe = sb("cbe", [P, 4, 4], F32, over)
        ckd = sb("ckd", [P, 4, 4], F32, over)
        absy, rn = cy[:, 0, :], cy[:, 1, :]
        egl = sb("egl", [P, 4, 8], F32, over)
        soft = sb("soft", [P, 2, 3, 2], F32, over)
        nega = sb("nega", [P, 1], F32, over)
        over.close()

        proj = ctx.enter_context(nc.psum_tensor("proj", [P, BANKS, S], F32))
        aux = ctx.enter_context(nc.psum_tensor("aux", [P, 4, S], F32))

        loaded = [sem("loaded0"), sem("loaded1")]
        set_up = sem("set_up")
        x_loaded = [sem(f"x_loaded{h}") for h in range(4)]
        stored = sem("stored")
        stage_free = sem("stage_free")
        hi_done = sem("hi_done")
        slot_free = sem("slot_free")
        taken = sem("taken")
        sq_done = sem("sq_done")
        xh_done = sem("xh_done")
        xl_done = sem("xl_done")
        ssum_done = sem("ssum_done")
        stat_done = sem("stat_done")
        std_done = sem("std_done")
        prod_done = sem("prod_done")
        ah_done = sem("ah_done")
        al_done = sem("al_done")
        silu_done = sem("silu_done")
        gate_done = sem("gate_done")
        x_done = sem("x_done")
        pos_loaded = sem("pos_loaded")
        angle_done = sem("angle_done")
        cs_done = sem("cs_done")
        norm_done = sem("norm_done")
        lat_done = sem("lat_done")
        mul_done = sem("mul_done")
        lath_done = sem("lath_done")
        extra_done = sem("extra_done")
        scores_done = sem("scores_done")
        bias_done = sem("bias_done")
        exp_done = sem("exp_done")
        probs_done = sem("probs_done")
        turned = sem("turned")
        pt_done = sem("pt_done")
        heads_done = sem("heads_done")
        og_done = sem("og_done")
        z_taken = sem("z_taken")
        ready = sem("ready")
        dve_step = sem("dve_step")
        consts2_loaded = sem("consts2_loaded")
        conv_done = sem("conv_done")
        heads_in = sem("heads_in")
        mix_pe, mix_dve, mix_act = sem("mix_pe"), sem("mix_dve"), sem("mix_act")

        PE_STEP, DVE_STEP, ACT_STEP = (Steps(names) for names in mixer_steps())

        def banks(i):
            return proj[:, i, :] if i < BANKS else aux[:, i - BANKS, :]

        def blocks_of(ap):
            return ap.rearrange("p (b k) -> p b k", k=P)

        def level(l):
            return consts2[:, l * P:l * P + P].unsqueeze(1).broadcast_to([P, 4, P])

        def head_bank(h, i):
            return (aux if i == 0 else proj)[:, h, :]

        def decay_of(h):
            return blocks_of(decay[:, h, :])

        def pair_of(k):
            tl, qb = k // 4, k % 4
            first = max(qb - 1, 0) if tl < 2 else 0
            return tl, qb, first * P, (qb + 1 - first) * P

        def pair_scores(k):
            tl, _, _, w = pair_of(k)
            if tl < 2:
                return aux[:, 2 * (k % 2), :].rearrange("p (t n) -> p t n", t=2)[:, :, 0:w]
            return aux[:, 2 * (k % 2):2 * (k % 2) + 2, 0:w]

        block = ctx.enter_context(nc.Block())

        def par(name, f):
            at = f + PARAMS[name]
            return params[:, bass.ds(at, 1)]

        def con(name, n=1, at=0):
            return consts[:, CONSTS[name] + at:CONSTS[name] + at + n]

        def split_after(n):
            return n + 1 < len(phases) and phases[n + 1] != "final"

        units = n_units(phases)
        assert units % RING in (0, 2)

        @block.sync
        def _(sp):
            for h in range(2):
                sp.dma_start(x[:, 2 * h:2 * h + 2, :], x_in[:, 2 * h:2 * h + 2, :]).then_inc(x_loaded[h], 16)
            def load(i, pair):
                sp.wait_ge(stage_free, i * RING + (2 * pair + 2))
                sp.dma_start(w_stage[:, 2 * pair:2 * pair + 2, :], stream[i * 2 + pair, :, :].rearrange("p (u n) -> p u n", u=2)).then_inc(loaded[pair], 16)

            with sp.Fori(0, units // RING) as i:
                load(i, 0)
                load(i, 1)
            if units % RING:
                load(units // RING, 0)
            if phases[-1] == "ffn":
                done = x_updates(phases)
                for h in range(4):
                    sp.wait_ge(x_done, DT * done - DT + 2 * h + 2)
                    sp.dma_start(out[:, 2 * h:2 * h + 2, :], x[:, 2 * h:2 * h + 2, :]).then_inc(stored, 16)
                sp.wait_ge(stored, 64)
            else:
                sp.wait_ge(x_done, DT * x_updates(phases) + 1)
                sp.dma_start(out, x[:, :, :]).then_inc(stored, 16)
                sp.wait_ge(stored, 16)

        @block.gpsimd
        def _(pool):
            pool.memset(ones[:, :], 1.0).then_inc(stage_free, RING)

            def lo(i, s):
                pool.wait_ge(hi_done, i * RING + (s + 1))
                pool.tensor_tensor(w_lo[:, s, :], w_stage[:, s, :], w_hi[:, s, :].bitcast(F32),
                                   ALU.subtract).then_inc(stage_free, 1)

            with pool.Fori(0, units // RING) as i:
                for s in range(RING):
                    lo(i, s)
            for s in range(units % RING):
                lo(units // RING, s)

        @block.tensor
        def _(pe):
            unit, tile = Count(), Count()
            al = Count()
            squares = Count()

            def products(bank, blocks, rhs, first_wait=None, hold=False):
                if bank is None:
                    o = aux[:, 0, :]
                else:
                    o = proj[:, bank, :]
                    pe.wait_ge(taken, tile.now(1))
                for b in range(blocks):
                    if b % 4 == 0:
                        pe.wait_ge(stage_free, unit.now(1 + RING))
                        slot = unit.n % RING
                    if first_wait is not None:
                        first_wait(b)
                    cols = slice(b % 4 * P, b % 4 * P + P)
                    hi, lo = rhs(b)
                    pe.matmul(o, w_hi[:, slot, cols], hi, start=(b == 0), stop=False)
                    pe.matmul(o, w_hi[:, slot, cols], lo, start=False, stop=False)
                    mm = pe.matmul(o, w_lo[:, slot, cols], hi, start=False, stop=(b == blocks - 1))
                    if (b % 4 == 3 or b == blocks - 1) and not hold:
                        mm.then_inc(slot_free, 1)
                        unit.up()
                if bank is not None:
                    tile.up()

            def of_x(k):
                return xh[:, k, :], xl[:, k, :]

            def of_act(k):
                return act_h[:, k, :], act_l[:, k, :]

            def first_tiles():
                if not side_by_side[0]:
                    products(tile.n % BANKS, 8, of_x, lambda k: pe.wait_ge(xl_done, 8 * x_norms[0] + k + 1))
                    stats()
                    for t in range(TOGETHER - 1):
                        products(tile.n % BANKS, 8, of_x)
                    return
                pe.wait_ge(taken, tile.now(TOGETHER))
                for k in range(DT):
                    pe.wait_ge(xl_done, 8 * x_norms[0] + k + 1)
                    for t in range(TOGETHER):
                        b = k * TOGETHER + t
                        if b % 4 == 0:
                            pe.wait_ge(stage_free, unit.now(1 + RING))
                        o, slot, cols = proj[:, (tile.n + t) % BANKS, :], unit.n % RING, slice(b % 4 * P, b % 4 * P + P)
                        pe.matmul(o, w_hi[:, slot, cols], xh[:, k, :], start=(k == 0), stop=False)
                        pe.matmul(o, w_hi[:, slot, cols], xl[:, k, :], start=False, stop=False)
                        mm = pe.matmul(o, w_lo[:, slot, cols], xh[:, k, :], start=False, stop=(k == DT - 1))
                        if b % 4 == 3:
                            mm.then_inc(slot_free, 1)
                            unit.up()
                tile.up(TOGETHER)
                stats()

            def project_in(tiles):
                first_tiles()
                products(tile.n % BANKS, 8, of_x)
                with Rolled(pe, tiles // 4 - 1, {unit: 8, tile: 4}):
                    for t in range(4):
                        products(tile.n % BANKS, 8, of_x)
                for t in range(tiles % 4):
                    products(tile.n % BANKS, 8, of_x)

            def project_out(k_tiles, per_tile, al_first):
                with Rolled(pe, DT // 4, {unit: 4 * per_tile, tile: 4}):
                    for t in range(4):
                        products(tile.n % BANKS, k_tiles, of_act, (lambda k: pe.wait_ge(al_done, al_first + k + 1)) if t == 0 else None)

            x_norms = [-1 if phases[0] == "final" else 0]

            side_by_side = [phases[0] in GROUPED]

            def stats():
                pe.wait_ge(ssum_done, squares.up(DT))
                pe.matmul(aux[:, 0, :], ones[:, :], ssum[:, :], start=True, stop=True).then_inc(stat_done, 1)

            def latent_attention():
                first_tiles()
                for t in range(3):
                    products(tile.n % BANKS, 8, of_x)
                squares.up(5)
                pe.wait_ge(norm_done, 1)
                pe.matmul(aux[:, 0, :], ones[:, :], ssum[:, :], start=True, stop=True).then_inc(stat_done, 1)
                pe.wait_ge(norm_done, 2)
                pe.matmul(aux[:, 1, :], ones[:, :], sum_kv[:, :], start=True, stop=True).then_inc(stat_done, 1)
                with Rolled(pe, 2, {unit: 8, tile: 4}):
                    for t in range(4):
                        products(tile.n % BANKS, 8, of_x)
                pe.wait_ge(norm_done, 3)
                pe.matmul(aux[:, 2, :], con("fold", P), tk[:, :], start=True, stop=True).then_inc(extra_done, 1)
                pe.wait_ge(lat_done, 5)
                of_lat = lambda first: (lambda k: (lat_h[:, first + k, :], lat_l[:, first + k, :]))

                def kv_tokens():
                    pe.wait_ge(taken, tile.now(1))
                    bank, slot = tile.n % BANKS, unit.n % RING
                    for blk in range(4):
                        toks = slice(blk * P, blk * P + P)
                        o = proj[:, bank, toks]
                        for k in range(2):
                            cols = slice((2 + k) * P, (3 + k) * P)
                            pe.matmul(o, lat_h[:, 3 + k, toks], w_hi[:, slot, cols], start=(k == 0), stop=False)
                            pe.matmul(o, lat_l[:, 3 + k, toks], w_hi[:, slot, cols], start=False, stop=False)
                            mm = pe.matmul(o, lat_h[:, 3 + k, toks], w_lo[:, slot, cols], start=False, stop=(k == 1))
                    mm.then_inc(slot_free, 1)
                    unit.up()
                    tile.up()

                def q_up():
                    products(tile.n % BANKS, 3, of_lat(0))

                def k_up():
                    products(tile.n % BANKS, 2, of_lat(3), hold=True)

                def scores(b, qb):
                    w = (qb + 1) * P
                    pe.wait_ge(exp_done, ex.now(1))
                    ex.up()
                    q, o = slice(qb * P, w), aux[:, 1 + qb % 2, 0:w]
                    pe.matmul(o, qn[:, b, q], kn[:, b, 0:w], start=True, stop=False)
                    pe.matmul(o, qr[:, b, q], k_rot[:, 0:w], start=False, stop=True).then_inc(scores_done, 1)

                def turn(qb):
                    pe.wait_ge(probs_done, tr.now(1))
                    pe.wait_ge(pt_done, tr.now(1))
                    tr.up()
                    at = qb * (qb + 1) // 2
                    for kb in range(qb + 1):
                        mm = pe.transpose(aux[:, 3, kb * P:kb * P + P], pr[:, at + kb, :], con("ident", P))
                    mm.then_inc(turned, 1)

                def head(b, nxt, z):
                    if nxt:
                        q_up()
                    turn(0)
                    scores(b, 2)
                    if nxt:
                        q_up()
                    turn(1)
                    scores(b, 3)
                    turn(2)
                    if nxt:
                        k_up()
                        kv_tokens()
                    if z:
                        pe.wait_ge(og_done, heads.now())
                        products(None, 8, of_x)
                        z_tiles.up()
                    turn(3)
                    if nxt:
                        first_scores(1 - b)
                    if z:
                        pe.wait_ge(z_taken, z_tiles.now(1))
                    pe.wait_ge(pt_done, tr.now(1))
                    for qb in range(4):
                        for kb in range(qb + 1):
                            mm = pe.matmul(aux[:, 0, qb * P:qb * P + P], vt[:, b, kb * P:kb * P + P],
                                           pt[:, qb * (qb + 1) // 2 + kb, :], start=(kb == 0), stop=(kb == qb))
                    mm.then_inc(heads_done, 1)
                    heads.up()

                def first_scores(b):
                    pe.wait_ge(taken, tile.now(-1) + BANKS)
                    scores(b, 0)
                    scores(b, 1)

                ex, tr, z_tiles, heads = Count(), Count(), Count(), Count()
                q_up(); q_up(); k_up(); kv_tokens()
                first_scores(0)
                with Rolled(pe, 7, {unit: 8, tile: 8, ex: 8, tr: 8, z_tiles: 1, heads: 2}):
                    head(0, True, False)
                    head(1, True, True)
                head(0, True, False)
                head(1, False, True)

            def made(ins, name):
                ins.then_inc(mix_pe, 1)
                PE_STEP.next(name)

            def spread_row(h, b, row):
                return pe.matmul(head_bank(h, b), consts[0:64, CONSTS["ident"] + row:CONSTS["ident"] + row + 1]
                                 .broadcast_to([64, P]), rows[0:64, :], start=True, stop=True)

            def per_block(h, b, stationary, moving, turn=False):
                for blk in range(4):
                    o = blocks_of(head_bank(h, b))[:, blk, :]
                    if turn:
                        mm = pe.transpose(o, moving(blk), con("ident", P))
                    else:
                        mm = pe.matmul(o, stationary(blk), moving(blk), start=True, stop=True)
                return mm

            def tiles(n):
                for _ in range(n):
                    products(tile.n % BANKS, 8, of_x)

            def delta_products():
                tiles(2)
                pe.wait_ge(heads_in, 20)
                for h in HEADS:
                    made(pe.matmul(head_bank(h, 0), ones[:, :], squares8[:, h, :], start=True, stop=True), ("ssk", h))
                tiles(1)
                for h in HEADS:
                    pe.wait_ge(mix_act, ACT_STEP["sk", h])
                    made(pe.matmul(head_bank(h, 0), ones[:, :], squares8[:, 4 + h, :], start=True, stop=True), ("ssq", h))
                tiles(1)
                pe.wait_ge(mix_dve, DVE_STEP["g"])
                pe.wait_ge(mix_act, ACT_STEP["sq", 3])
                for blk in range(4):
                    mm = pe.transpose(head_bank(0, 0)[:, blk * 68:blk * 68 + 68], rows[0:68, blk * P:blk * P + P],
                                      consts[0:68, CONSTS["ident"]:CONSTS["ident"] + 68])
                made(mm, "rowt")
                tiles(3)
                for h in HEADS:
                    if h == 0:
                        pe.wait_ge(mix_dve, DVE_STEP["cols"])
                    made(spread_row(h, 0, h), ("bb", h))
                tiles(1)
                for h in HEADS:
                    pe.wait_ge(mix_dve, DVE_STEP["kb", h])
                    made(spread_row(h, 0, 32 + h), ("bg", h))
                tiles(1)
                for h in HEADS:
                    pe.wait_ge(mix_act, ACT_STEP["egl", h])
                    made(per_block(h, 0, None, lambda blk: vf[:, h, blk * P:blk * P + P], turn=True), ("vt", h))
                tiles(1)
                for h in HEADS:
                    pe.wait_ge(mix_act, ACT_STEP["vb", h])
                    made(per_block(h, 0, None, lambda blk: kf[:, h, blk * P:blk * P + P], turn=True), ("kt", h))
                tiles(1)
                for h in HEADS:
                    pe.wait_ge(mix_act, ACT_STEP["kd", h])
                    made(per_block(h, 0, lambda blk: kf[:, h, blk * P:blk * P + P],
                                   lambda blk: kb[:, h, blk * P:blk * P + P]), ("g1", h))
                tiles(1)
                for h in HEADS:
                    pe.wait_ge(mix_dve, DVE_STEP["lt", h])
                    made(per_block(h, 0, lambda blk: kf[:, h, blk * P:blk * P + P],
                                   lambda blk: qf[:, h, blk * P:blk * P + P]), ("g2", h))
                tiles(2)

            def inverse():
                for h in HEADS:
                    pe.wait_ge(mix_dve, DVE_STEP["at", h])
                    made(per_block(h, 0, None, lambda blk: xt[:, h, blk, :], turn=True), ("x1", h))
                pe.wait_ge(taken, tile.now() + BANKS)
                for h in HEADS:
                    made(spread_row(h, 1, 32 + h), ("bg2", h))
                for l in range(1, LEVELS):
                    for h in HEADS:
                        if l == 1:
                            pe.wait_ge(mix_act, ACT_STEP["xc", h])
                            pe.wait_ge(mix_dve, DVE_STEP["qd", h])
                        else:
                            pe.wait_ge(mix_dve, DVE_STEP[f"xt{l - 1}", h])
                        made(per_block(h, 1, lambda blk: e_mat[:, h, blk, :], lambda blk: x_mat[:, h, blk, :]), (f"y{l}", h))
                    for h in HEADS:
                        pe.wait_ge(mix_act, ACT_STEP[f"yc{l}", h])
                        mm = per_block(h, 0, lambda blk: y_mat[:, h, blk, :], lambda blk: xt[:, h, blk, :])
                        if l < LEVELS - 1:
                            mm = per_block(h, 1, lambda blk: xt[:, h, blk, :], lambda blk: y_mat[:, h, blk, :])
                        made(mm, (f"p{l}", h))
                for h in HEADS:
                    pe.wait_ge(mix_dve, DVE_STEP[f"xt{LEVELS - 1}", h])
                    made(per_block(h, 0, lambda blk: blocks_of(vf[:, h, :])[:, blk, :],
                                   lambda blk: xt[:, h, blk, :]), ("wt", h))

            def chunk(c):
                blk, r = c // 2, CHUNK * (c % 2)
                toks = slice(c * CHUNK, c * CHUNK + CHUNK)
                if c:
                    pe.wait_ge(mix_dve, DVE_STEP["st", c - 1])
                for h in HEADS:
                    o = banks(0)[r:r + CHUNK, h * P:h * P + P]
                    mm = pe.matmul(o, xt[:, h, blk, r:r + CHUNK], vbeta[:, h, blk, :], start=(h == 0), stop=(c == 0),
                                   skip_group_check=True)
                    if c:
                        mm = pe.matmul(o, vf[:, h, toks], state[:, h, :], start=False, stop=True,
                                       skip_group_check=True)
                made(mm, ("nv", c))
                turn(2 * c)
                if c:
                    pe.wait_ge(mix_act, ACT_STEP["mc", 2 * c - 3] if c > 1 else ACT_STEP["oc", 0])
                    for h in HEADS:
                        pe.matmul(banks(1)[:, h * CHUNK:h * CHUNK + CHUNK], state[:, h, :], qf[:, h, toks],
                                  start=(h == 0), stop=False, skip_group_check=True)
                pe.wait_ge(mix_act, ACT_STEP["vn", c])
                for h in HEADS:
                    mm = pe.matmul(banks(1)[:, h * CHUNK:h * CHUNK + CHUNK], vnew[r:r + CHUNK, h * P:h * P + P],
                                   blocks_of(kf[:, h, :])[r:r + CHUNK, blk, r:r + CHUNK],
                                   start=(c == 0 and h == 0), stop=True, skip_group_check=True)
                made(mm, ("o", c))
                if c < CHUNKS - 1:
                    for h in HEADS:
                        mm = pe.matmul(banks(0)[:, h * P:h * P + P], kdec[r:r + CHUNK, h, blk, :],
                                       vnew[r:r + CHUNK, h * P:h * P + P], start=(h == 0), stop=True,
                                       skip_group_check=True)
                    made(mm, ("su", c))

            def attend(k):
                if k < PAIRS:
                    tl, qb, first, w = pair_of(k)
                    if k >= 2:
                        pe.wait_ge(mix_act, ACT_STEP["ex", k - 2])
                    for t in range(2):
                        head = 2 * (tl % 2) + t
                        if tl < 2:
                            part = slice(64 * (head // 2), 64 * (head // 2) + 64)
                            q, keys, dist, slope = a_q[part, head % 2, :], a_kv[part, 0, :], CONSTS2["dist_swa"] + 2 * P, head
                        else:
                            part = slice(64 * t, 64 * t + 64)
                            q, keys, dist, slope = b_q[part, tl - 2, :], b_k[part, tl - 2, :], CONSTS2["dist"] + 4 * P, 4 + head
                        o = pair_scores(k)[:, t, :]
                        pe.matmul(o, q[:, qb * P:qb * P + P], keys[:, first:first + w], start=True, stop=False)
                        mm = pe.matmul(o, slope_ident[:, slope, :], consts2[:, dist - w:dist], start=False, stop=True)
                    made(mm, ("s", k))

            def turn(k):
                if 1 <= k <= PAIRS:
                    k -= 1
                    w = pair_of(k)[3]
                    pe.wait_ge(mix_dve, DVE_STEP["nr", k])
                    if k:
                        pe.wait_ge(mix_act, ACT_STEP["pc", k - 1])
                    for t in range(2):
                        for kb_ in range(w // P):
                            mm = pe.transpose(banks(2 + t)[:, kb_ * P:kb_ * P + P],
                                              probs[:, k % 2, t, kb_ * P:kb_ * P + P], con("ident", P))
                    made(mm, ("t", k))

            def values(k):
                if k < 2:
                    return
                k -= 2
                tl, qb, first, w = pair_of(k)
                pe.wait_ge(mix_act, ACT_STEP["pc", k])
                pe.wait_ge(mix_act, max(ACT_STEP["oc", min(k // 2 + 1, CHUNKS - 1)], ACT_STEP["mc", k - 1] if k else 0))
                for t in range(2):
                    head = 2 * (tl % 2) + t
                    at = 64 * (head // 2) if tl < 2 else P + 64 * head
                    for kb_ in range(w // P):
                        mm = pe.matmul(banks(1)[64 * t:64 * t + 64, 2 * P:3 * P],
                                       v_tok[:, first // P + kb_, at // P, at % P:at % P + 64],
                                       probs_t[:, k % 2, t, kb_ * P:kb_ * P + P],
                                       start=(kb_ == 0), stop=(kb_ == w // P - 1), skip_group_check=True)
                made(mm, ("pv", k))

            def hybrid_mixer():
                project_in(13)
                delta_products()
                inverse()
                pe.wait_ge(mix_act, ACT_STEP["nw", 3])
                for blk in range(4):
                    if blk >= 2:
                        pe.wait_ge(mix_act, ACT_STEP["avc", blk - 2])
                    for i, v in enumerate((a_kv[:, 1, :], b_v[:, 0, :], b_v[:, 1, :])):
                        mm = pe.transpose(banks(4 * (blk % 2) + 1)[:, i * P:i * P + P], v[:, blk * P:blk * P + P], con("ident", P))
                    made(mm, ("av", blk))
                pe.wait_ge(mix_act, ACT_STEP["avc", 3])
                pe.wait_ge(mix_dve, DVE_STEP["slopes"])
                for c in range(CHUNKS):
                    attend(2 * c)
                    chunk(c)
                    values(2 * c)
                    attend(2 * c + 1)
                    turn(2 * c + 1)
                    if c % 2:
                        pe.wait_ge(mix_act, max(ACT_STEP["osq", c // 2], ACT_STEP["mc", 2 * c - 2]))
                        for h in HEADS:
                            col = 3 * P + 4 * (c // 2) + h
                            mm = pe.matmul(banks(1)[:, col:col + 1], osq[:, c // 2 % 2, h, :], ones[:, 0:1],
                                           start=True, stop=True, skip_group_check=True)
                        made(mm, ("osum", c // 2))
                    values(2 * c + 1)
                for k in (PAIRS, PAIRS + 1):
                    attend(k)
                    turn(k)
                    values(k)
                pe.wait_ge(mix_dve, DVE_STEP["orc"])
                for blk in range(4):
                    mm = pe.transpose(banks(0)[0:4, blk * P:blk * P + P], rc[:, blk * 4:blk * 4 + 4], con("ident", P))
                made(mm, "ornt")
                pe.wait_ge(mix_dve, DVE_STEP["orn"])
                for h in HEADS:
                    made(pe.matmul(banks(4 + h), consts[0:4, CONSTS["ident"] + h:CONSTS["ident"] + h + 1]
                                   .broadcast_to([4, P]), rn[0:4, :], start=True, stop=True), ("ob", h))

            pe.wait_ge(stage_free, RING)
            if phases[0] == "final":
                stats()
            for n, ph in enumerate(phases):
                if ph.startswith("pool"):
                    project_in(IT)
                    with Rolled(pe, 4, {unit: 12, tile: 8}) as g:
                        for t in range(4):
                            products(tile.n % BANKS, 8, of_x)
                        for t in range(4):
                            products(tile.n % BANKS, 4, lambda c: (act_h[:, g * 4 + (4 + c), :], act_l[:, g * 4 + (4 + c), :]),
                                     (lambda c: pe.wait_ge(al_done, al.n + IT)) if t == 0 else None)
                    project_out(IT, 4, al.n + IT)
                    al.up(2 * IT)
                if ph == "conv":
                    project_in(4 * IT)
                    project_out(IT, 4, al.n)
                    al.up(IT)
                if ph == "mla":
                    latent_attention()
                    project_out(IT, 4, al.n)
                    al.up(IT)
                if ph == "mixer":
                    hybrid_mixer()
                    project_out(DT, 2, al.n)
                    al.up(DT)
                    stats()
                if ph == "ffn":
                    project_in(2 * FT)
                    project_out(FT, 6, al.n)
                    al.up(FT)
                    stats()
                if split_after(n):
                    x_norms[0] += 1
                    side_by_side[0] = phases[n + 1] in GROUPED
                elif ph not in ("mixer", "ffn"):
                    stats()

        @block.scalar
        def _(act):
            unit, tile = Count(), Count()
            sqs, hs, stds, als, prods, silus, gates, xs = (Count() for _ in range(8))

            def his(n):
                for _ in range(n):
                    u = unit.n
                    pair = (u // 2) % 2
                    value = 16 * (u // RING + 1)
                    if unit.i is not None:
                        value = unit.i * (unit.per // RING * 16) + value
                    act.wait_ge(loaded[pair], value)
                    act.wait_ge(slot_free, unit.now(1))
                    act.activation(w_hi[:, u % RING, :], w_stage[:, u % RING, :], ACT.Copy).then_inc(hi_done, 1)
                    unit.up()

            def square(of):
                if sqs.n > 1:
                    act.wait_ge(ssum_done, sqs.now() - 1)
                act.activation(sq[:, sqs.n % 2, :], of, ACT.Square).then_inc(sq_done, 1)
                sqs.up()

            def residual_tile(f, gain):
                square(x[:, f, :])
                if gain:
                    act.activation(xh[:, f, :], x[:, f, :], ACT.Identity, scale=par(gain, f)).then_inc(xh_done, 1)
                    hs.up()

            def deviation(ahead):
                if ahead:
                    his(4)
                stds.up()
                act.wait_ge(stat_done, stds.n)
                act.activation(std[:, :], aux[:, 0, :], ACT.Sqrt, bias=con("eps"), scale=1.0 / D).then_inc(std_done, 1)

            def out_tiles(per_tile, gain, ahead):
                with Rolled(act, DT // 4, {unit: 4 * per_tile, tile: 4, sqs: 4, hs: 4 if gain else 0}) as i:
                    for t in range(4):
                        his(per_tile)
                        act.wait_ge(taken, tile.up() + BANKS)
                        residual_tile(i * 4 + t, gain)
                deviation(ahead)

            def out_tiles_of_y(per_tile):
                with Rolled(act, DT // 4, {unit: 4 * per_tile, tile: 4, sqs: 4}):
                    for t in range(4):
                        his(per_tile)
                        act.wait_ge(slot_free, unit.now())
                        square(proj[:, tile.n % BANKS, :])
                        tile.up()
                deviation(False)

            def updated_tiles(gain, ahead):
                for f in range(DT):
                    act.wait_ge(x_done, xs.up())
                    residual_tile(f, gain)
                    if ahead and f >= DT - 4:
                        his(1)
                deviation(False)

            def operand(slot, wait, value):
                act.wait_ge(wait, value)
                act.activation(act_h[:, slot, :], prod[:, :], ACT.Copy).then_inc(ah_done, 1)

            def latent_attention(gain):
                act.dma_start(pos_i[:, :], pos_in).then_inc(pos_loaded, 16)
                for t in range(5):
                    his(2)
                    if t == 3:
                        act.wait_ge(angle_done, 1)
                        act.activation(cs[:, :], angle[:, :], ACT.Sin).then_inc(cs_done, 1)
                    act.wait_ge(taken, tile.up() + BANKS)
                    square(lat[:, t, :])
                his(2)
                tile.up()
                his(2)
                for bank, n in ((0, 384), (1, 256)):
                    stds.up()
                    act.wait_ge(stat_done, stds.n)
                    if bank:
                        act.wait_ge(norm_done, 4)
                    act.activation(std[:, :], aux[:, bank, :], ACT.Sqrt, bias=con("eps"), scale=1.0 / n).then_inc(std_done, 1)
                for f in range(5):
                    if f in (1, 3):
                        his(2)
                    act.wait_ge(mul_done, f + 1)
                    gain_f = par("q_norm", f) if f < 3 else par("kv_norm", f - 3)
                    act.activation(lat_h[:, f, :], lat[:, f, :], ACT.Identity, scale=gain_f).then_inc(lath_done, 1)
                his(2)
                for t in range(8):
                    if t >= 4:
                        his(2)
                    act.wait_ge(taken, tile.up() + BANKS)
                    act.activation(zs[:, t, :], zs[:, t, :], ACT.Silu).then_inc(silu_done, 1)
                    silus.up()
                his(3)
                tile.up(4)

                def expo(qb):
                    at, n = qb * (qb + 1) // 2, qb + 1
                    act.wait_ge(bias_done, es.up())
                    act.activation(pr[:, at:at + n, :], aux[:, 1 + qb % 2, 0:n * P].rearrange("p (b k) -> p b k", k=P), ACT.Exp,
                                   bias=small[:, 4 + qb:5 + qb], scale=SCALE,
                                   accum_out=small[:, 8 + qb:9 + qb]).then_inc(exp_done, 1)

                def head(nxt, z):
                    if nxt:
                        his(1)
                    expo(2)
                    if nxt:
                        his(1)
                    expo(3)
                    if nxt:
                        his(1)
                        tile.up(4)
                    if z is not None:
                        his(2)
                        act.wait_ge(z_taken, zts.up() + 1)
                        act.activation(zs[:, z, :], zs[:, z, :], ACT.Silu).then_inc(silu_done, 1)
                        silus.up()
                    if nxt:
                        expo(0)
                        expo(1)

                es, zts = Count(), Count()
                expo(0)
                expo(1)
                with Rolled(act, 7, {unit: 8, tile: 8, es: 8, zts: 1, silus: 1}) as i:
                    head(True, None)
                    head(True, i)
                head(True, None)
                head(False, 7)
                for k in range(IT):
                    if k == 0:
                        act.wait_ge(og_done, IT)
                    act.activation(act_h[:, k, :], og[:, k, :], ACT.Copy).then_inc(ah_done, 1)

            def hybrid_mixer():
                act.dma_start(consts2[:, :], consts2_in).then_inc(consts2_loaded, 16)
                ins = Count()

                def conv_tile(n, to, square_to=None):
                    act.wait_ge(conv_done, n + 1)
                    act.activation(to, cy[:, n % 2, :], ACT.Silu).then_inc(heads_in, 1)
                    ins.up()
                    if square_to is not None:
                        act.wait_ge(heads_in, ins.now())
                        act.activation(square_to, to, ACT.Square).then_inc(heads_in, 1)
                        ins.up()

                for i in range(8):
                    his(FIRST_HIS[i])
                    tile.up()
                    conv_tile(i, kf[:, i, :] if i < 4 else qf[:, i - 4, :], squares8[:, i, :])
                his(2)
                tile.up()
                for i in range(4):
                    his(2)
                    tile.up()
                    conv_tile(8 + i, vf[:, i, :])

                def made(i, name):
                    i.then_inc(mix_act, 1)
                    act.wait_ge(mix_act, ACT_STEP.next(name))

                def his_of(tiles):
                    his(2 * tiles)
                    tile.up(tiles)

                his_of(1)
                act.wait_ge(mix_dve, DVE_STEP["ydt"])
                made(act.activation(raw[0:4, :], raw[0:4, :], ACT.Tanh, scale=0.5), "tanh")
                made(act.activation(absy[32:36, :], absy[32:36, :], ACT.Exp, scale=-1.0), "e1")
                made(act.activation(absy[32:36, :], absy[32:36, :], ACT.Ln, bias=ones[32:36, 0:1]), "ln")
                made(act.activation(nega[32:36, :], params[32:36, PARAMS["a_log"]:PARAMS["a_log"] + 1], ACT.Exp), "nega")
                his_of(1)
                for h in HEADS:
                    act.wait_ge(mix_pe, PE_STEP["ssk", h])
                    made(act.activation(squares8[:, h, :], head_bank(h, 0), ACT.Sqrt, bias=con("eps")), ("sk", h))
                his_of(1)
                for h in HEADS:
                    act.wait_ge(mix_pe, PE_STEP["ssq", h])
                    made(act.activation(squares8[:, 4 + h, :], head_bank(h, 0), ACT.Sqrt, bias=con("eps")), ("sq", h))
                his_of(3)
                for h in HEADS:
                    act.wait_ge(taken, tile.now() - 5 + h + BANKS)
                    made(act.activation(zc[:, h, :], zc[:, h, :], ACT.Silu), ("zs", h))
                act.wait_ge(mix_dve, DVE_STEP["cols"])
                made(act.activation(ceg[:, :, :], cols[:, :, 32:36], ACT.Exp), "cexp")
                his_of(2)
                act.wait_ge(mix_dve, DVE_STEP["cd"])
                made(act.activation(ckd[:, :, :], ckd[:, :, :], ACT.Exp), "ckd")
                for h in HEADS:
                    act.wait_ge(mix_dve, DVE_STEP["dt", h])
                    made(act.activation(egl[:, h, :], head_bank(h, 0)[:, CHUNK - 1::CHUNK], ACT.Exp), ("egl", h))
                    made(act.activation(decay[:, h, :], decay[:, h, :], ACT.Exp), ("edt", h))
                his_of(1)
                for h in HEADS:
                    act.wait_ge(mix_pe, PE_STEP["vt", h])
                    for blk in range(4):
                        ins = act.activation(vbeta[:, h, blk, :], head_bank(h, 0)[:, blk * P:blk * P + P], ACT.Copy,
                                             scale=cols[:, blk, h:h + 1])
                    made(ins, ("vb", h))
                his_of(1)
                for h in HEADS:
                    act.wait_ge(mix_dve, DVE_STEP["kbe", h])
                    for blk in range(4):
                        ins = act.activation(kdec[:, h, blk, :], head_bank(h, 0)[:, blk * P:blk * P + P], ACT.Copy,
                                             scale=ckd[:, blk, h:h + 1])
                    made(ins, ("kd", h))
                his_of(4)
                for h in HEADS:
                    act.wait_ge(mix_pe, PE_STEP["x1", h])
                    made(act.activation(x_mat[:, h, :, :], blocks_of(head_bank(h, 0)), ACT.Copy), ("xc", h))
                for h in HEADS:
                    act.wait_ge(mix_pe, PE_STEP["bg2", h])
                    made(act.activation(eg[:, h, :, :], blocks_of(head_bank(h, 1)), ACT.Exp), ("eg", h))
                for l in range(1, LEVELS):
                    for h in HEADS:
                        act.wait_ge(mix_pe, PE_STEP[f"y{l}", h])
                        made(act.activation(y_mat[:, h, :, :], blocks_of(head_bank(h, 1)), ACT.Copy), (f"yc{l}", h))
                for h in HEADS:
                    act.wait_ge(mix_pe, PE_STEP["wt", h])
                    made(act.activation(vf[:, h, :], head_bank(h, 0), ACT.Copy, scale=-1.0), ("nw", h))
                for blk in range(4):
                    act.wait_ge(mix_pe, PE_STEP["av", blk])
                    made(act.activation(v_tok[:, blk, :, :], blocks_of(banks(4 * (blk % 2) + 1)[:, 0:3 * P]), ACT.Copy), ("avc", blk))

                def attend(k):
                    if k < PAIRS:
                        tl, qb, first, w = pair_of(k)
                        act.wait_ge(mix_dve, DVE_STEP["mx", k])
                        for t in range(2):
                            e = act.activation(probs[:, k % 2, t, 0:w], pair_scores(k)[:, t, :], ACT.Exp,
                                               bias=soft[:, k % 2, 0, t:t + 1], accum_out=soft[:, k % 2, 1, t:t + 1])
                        if tl < 2:
                            e = act.activation(soft[:, k % 2, 2, :], soft[:, k % 2, 2, :], ACT.Exp)
                        made(e, ("ex", k))

                def turn(k):
                    if 1 <= k <= PAIRS:
                        k -= 1
                        w = pair_of(k)[3]
                        act.wait_ge(mix_pe, PE_STEP["t", k])
                        made(act.activation(probs_t[:, k % 2, :, 0:w], proj[:, 2:4, 0:w], ACT.Copy), ("pc", k))

                def values(k):
                    if k < 2:
                        return
                    k -= 2
                    tl, qb = k // 4, k % 4
                    act.wait_ge(mix_pe, PE_STEP["pv", k])
                    made(act.activation(mixed[:, tl, qb * P:qb * P + P], banks(1)[:, 2 * P:3 * P], ACT.Copy), ("mc", k))

                for c in range(CHUNKS):
                    r = CHUNK * (c % 2)
                    act.wait_ge(mix_pe, PE_STEP["nv", c])
                    made(act.activation(vnew[r:r + CHUNK, :], banks(0)[r:r + CHUNK, :], ACT.Copy), ("vn", c))
                    attend(2 * c)
                    turn(2 * c)
                    act.wait_ge(mix_pe, PE_STEP["o", c])
                    made(act.activation(mixed[:, 4:8, c * CHUNK:c * CHUNK + CHUNK],
                                        banks(1)[:, 0:4 * CHUNK].rearrange("p (h k) -> p h k", k=CHUNK), ACT.Copy), ("oc", c))
                    if c % 2:
                        toks = slice(c // 2 * P, c // 2 * P + P)
                        made(act.activation(osq[:, c // 2 % 2, :, :], mixed[:, 4:8, toks], ACT.Square), ("osq", c // 2))
                    values(2 * c)
                    attend(2 * c + 1)
                    turn(2 * c + 1)
                    values(2 * c + 1)
                for k in (PAIRS, PAIRS + 1):
                    attend(k)
                    turn(k)
                    values(k)
                made(act.activation(rc[:, :], banks(1)[:, 3 * P:3 * P + 16], ACT.Sqrt, bias=con("eps"), scale=1.0 / P), "osqrt")
                for k in range(DT):
                    if k >= 4:
                        act.wait_ge(mix_dve, DVE_STEP["on", k - 4])
                    act.activation(act_h[:, k, :], mixed[:, k, :], ACT.Copy).then_inc(ah_done, 1)

            act.dma_start(params[:, :], params_in).then_inc(set_up, 16)
            act.dma_start(consts[:, :], consts_in).then_inc(set_up, 16)
            for h in (2, 3):
                act.dma_start(x[:, 2 * h:2 * h + 2, :], x_in[:, 2 * h:2 * h + 2, :]).then_inc(x_loaded[h], 16)
            act.wait_ge(set_up, 32)
            for f in range(DT):
                act.wait_ge(x_loaded[f // 2], 16)
                residual_tile(f, phases[0] != "final" and NORM_OF[phases[0]])
                if f in (2, 5):
                    his(2)
            deviation(phases[0] in GROUPED)
            for n, ph in enumerate(phases):
                nxt = NORM_OF[phases[n + 1]] if split_after(n) else None
                ahead = split_after(n) and phases[n + 1] in GROUPED
                if ph.startswith("pool"):
                    with Rolled(act, 4, {unit: 8, tile: 4, prods: 4}) as g:
                        for t in range(4):
                            his(2)
                            tile.up()
                            operand(g * 4 + (4 + t), prod_done, prods.up())
                    with Rolled(act, 4, {unit: 12, tile: 8, silus: 4}) as g:
                        for t in range(4):
                            his(2)
                            act.wait_ge(taken, tile.up() + BANKS)
                            act.activation(z4[:, t, :], z4[:, t, :], ACT.Silu).then_inc(silu_done, 1)
                            silus.up()
                        for t in range(4):
                            his(1)
                            operand(g * 4 + t, taken, tile.up() + BANKS)
                    out_tiles(4, nxt, ahead)
                if ph == "conv":
                    with Rolled(act, IT, {unit: 8, tile: 4, silus: 1, prods: 1}) as f:
                        his(8)
                        tile.up(4)
                        act.wait_ge(taken, tile.now() + BANKS)
                        act.activation(zb[:, :], zb[:, :], ACT.Silu).then_inc(silu_done, 1)
                        silus.up()
                        operand(f, prod_done, prods.up())
                    out_tiles(4, nxt, ahead)
                if ph == "mla":
                    latent_attention(nxt)
                    out_tiles(4, nxt, ahead)
                if ph == "final":
                    updated_tiles(nxt, ahead)
                if ph == "mixer":
                    hybrid_mixer()
                    out_tiles_of_y(2)
                    if nxt:
                        updated_tiles(nxt, ahead)
                if ph == "ffn":
                    def gated(f, units=4):
                        his(units)
                        tile.up(2)
                        act.wait_ge(gate_done, gates.up())
                        act.activation(yg[:, 0, :], yg[:, 0, :], ACT.Gelu_apprx_tanh).then_inc(silu_done, 1)
                        silus.up()
                        operand(f, prod_done, prods.up())

                    gated(0, 2)
                    gated(1, 2)
                    with Rolled(act, FT // 2 - 1, {unit: 8, tile: 4, gates: 2, silus: 2, prods: 2}) as i:
                        for t in range(2):
                            gated(i * 2 + (2 + t))
                    out_tiles_of_y(6)

        @block.vector
        def _(dve):
            unit, tile, step = Count(), Count(), Count()
            sqs, hs, stds, prods, als, silus, gates, xs = (Count() for _ in range(8))

            def link(ins):
                ins.then_inc(dve_step, 1)
                dve.wait_ge(dve_step, step.up())

            def bank(n_units):
                unit.up(n_units)
                dve.wait_ge(slot_free, unit.now() + RING)
                return proj[:, tile.n % BANKS, :]

            def take(ins):
                ins.then_inc(taken, 1)
                dve.wait_ge(taken, tile.up() + BANKS)

            def add_square():
                dve.wait_ge(sq_done, sqs.up())
                dve.tensor_tensor(ssum[:, :], ssum[:, :], sq[:, (sqs.n - 1) % 2, :], ALU.add).then_inc(ssum_done, 1)
                dve.wait_ge(ssum_done, sqs.now())

            def residual_tile(f, gain):
                add_square()
                if gain:
                    dve.wait_ge(xh_done, hs.up())
                    dve.scalar_tensor_tensor(xl[:, f, :], x[:, f, :], par(gain, f), xh[:, f, :].bitcast(F32),
                                             ALU.mult, ALU.subtract).then_inc(xl_done, 1)

            def deviation():
                stds.up()
                dve.wait_ge(stat_done, stds.n)
                link(dve.memset(ssum[:, :], 0.0))
                dve.wait_ge(std_done, stds.n)
                link(dve.reciprocal(rstd[:, :], std[:, :]))

            def out_tiles(per_tile, gain):
                with Rolled(dve, DT // 4, {unit: 4 * per_tile, tile: 4, sqs: 4, hs: 4 if gain else 0}) as i:
                    for t in range(4):
                        f = i * 4 + t
                        take(dve.tensor_tensor(x[:, f, :], bank(per_tile), x[:, f, :], ALU.add))
                        residual_tile(f, gain)
                deviation()

            def out_tiles_of_y(per_tile, post):
                with Rolled(dve, DT // 4, {unit: 4 * per_tile, tile: 4, sqs: 4}) as i:
                    for t in range(4):
                        b = bank(per_tile)
                        add_square()
                        take(dve.tensor_scalar(y[:, i * 4 + t, :], b, par(post, i * 4 + t), None, ALU.mult))
                deviation()

            def add_normed(gain):
                for f in range(DT):
                    link(dve.tensor_tensor(y[:, f, :], y[:, f, :], rstd[:, :], ALU.mult))
                    dve.tensor_tensor(x[:, f, :], x[:, f, :], y[:, f, :], ALU.add).then_inc(x_done, 1)
                    dve.wait_ge(x_done, xs.up())
                    if gain and f:
                        residual_tile(f - 1, gain)
                if gain:
                    residual_tile(DT - 1, gain)
                if gain:
                    deviation()

            def rest(slot):
                als.up()
                dve.wait_ge(ah_done, als.now())
                dve.tensor_tensor(act_l[:, slot, :], prod[:, :], act_h[:, slot, :].bitcast(F32),
                                  ALU.subtract).then_inc(al_done, 1)
                dve.wait_ge(al_done, als.now())

            def angles():
                dve.wait_ge(pos_loaded, 16)
                link(dve.tensor_copy(turns[:, :], pos_i[:, :]))
                link(dve.tensor_scalar(angle[:, :], turns[:, :], con("freq"), None, ALU.mult))
                link(dve.tensor_scalar(turns_i[:, :], angle[:, :], con("phase"), 1.0 / TWO_PI, ALU.add, ALU.mult))
                link(dve.tensor_copy(turns[:, :], turns_i[:, :]))
                for part in TWO_PI_PARTS:
                    link(dve.scalar_tensor_tensor(angle[:, :], turns[:, :], -part, angle[:, :], ALU.mult, ALU.add))
                link(dve.tensor_scalar(angle[:, :], angle[:, :], con("phase"), 3.1415925, ALU.add, ALU.min))
                dve.tensor_scalar(angle[:, :], angle[:, :], -3.1415925, None, ALU.max).then_inc(angle_done, 1)

            def latent_attention():
                for t in range(5):
                    take(dve.tensor_tensor(lat[:, t, :], bank(2), rstd[:, :], ALU.mult))
                    dve.wait_ge(sq_done, sqs.up())
                    total = ssum if t < 3 else sum_kv
                    if t == 3:
                        dve.tensor_copy(total[:, :], sq[:, (sqs.n - 1) % 2, :]).then_inc(ssum_done, 1)
                    else:
                        dve.tensor_tensor(total[:, :], total[:, :], sq[:, (sqs.n - 1) % 2, :], ALU.add).then_inc(ssum_done, 1)
                    dve.wait_ge(ssum_done, sqs.now())
                    if t in (2, 4):
                        dve.memset(small[:, 0:1], 0.0).then_inc(norm_done, 1)
                        dve.wait_ge(norm_done, 1 if t == 2 else 2)
                    if t == 1:
                        angles()
                take(dve.tensor_tensor(tk[:, :], bank(2), rstd[:, :], ALU.mult))
                dve.wait_ge(cs_done, 1)
                dve.tensor_tensor(tk[:, :], tk[:, :], cs[:, :], ALU.mult).then_inc(norm_done, 1)
                for part, fs in enumerate((range(3), range(3, 5))):
                    stds.up()
                    dve.wait_ge(std_done, stds.n)
                    r = dve.reciprocal(rlat[:, :], std[:, :])
                    if part == 0:
                        r.then_inc(norm_done, 1)
                        dve.wait_ge(norm_done, 4)
                    else:
                        link(r)
                    for f in fs:
                        dve.tensor_tensor(lat[:, f, :], lat[:, f, :], rlat[:, :], ALU.mult).then_inc(mul_done, 1)
                        dve.wait_ge(mul_done, f + 1)
                link(dve.memset(ssum[:, :], 0.0))
                for f in range(5):
                    gain_f = par("q_norm", f) if f < 3 else par("kv_norm", f - 3)
                    dve.wait_ge(lath_done, f + 1)
                    dve.scalar_tensor_tensor(lat_l[:, f, :], lat[:, f, :], gain_f, lat_h[:, f, :].bitcast(F32),
                                             ALU.mult, ALU.subtract).then_inc(lat_done, 1)
                for t in range(8):
                    take(dve.tensor_tensor(zs[:, t, :], bank(2), rstd[:, :], ALU.mult))
                dve.wait_ge(extra_done, 1)
                dve.tensor_copy(k_rot[:, :], aux[:, 2, :]).then_inc(z_taken, 1)
                dve.wait_ge(z_taken, 1)

                def take_qn(b):
                    take(dve.tensor_copy(qn[:, b, :], bank(1)))

                def take_qr(b):
                    take(dve.tensor_tensor(qr[:, b, :], bank(1), cs[:, :], ALU.mult))

                def take_kn(b):
                    take(dve.tensor_copy(kn[:, b, :], bank(1)))

                def take_vt(b):
                    take(dve.tensor_copy(vt[:, b, :], bank(0)))

                def row_max(qb):
                    dve.wait_ge(scores_done, sc.up())
                    s = aux[:, 1 + qb % 2, 0:qb * P + P]
                    link(dve.tensor_tensor(s[:, qb * P:], s[:, qb * P:], con("causal", P), ALU.add))
                    link(dve.tensor_reduce(small[:, qb:qb + 1], s, AX.X, ALU.max))
                    dve.tensor_scalar(small[:, 4 + qb:5 + qb], small[:, qb:qb + 1], -SCALE, None, ALU.mult).then_inc(bias_done, 1)
                    bs.up()

                def normal(qb):
                    at, n = qb * (qb + 1) // 2, qb + 1
                    dve.wait_ge(exp_done, en.up() + 2)
                    link(dve.reciprocal(small[:, 12 + qb:13 + qb], small[:, 8 + qb:9 + qb]))
                    dve.tensor_scalar(pr[:, at:at + n, :], pr[:, at:at + n, :], small[:, 12 + qb:13 + qb], None, ALU.mult).then_inc(probs_done, 1)

                def copy_turned(qb):
                    at, n = qb * (qb + 1) // 2, qb + 1
                    dve.wait_ge(turned, tn.up())
                    dve.tensor_copy(pt[:, at:at + n, :], aux[:, 3, 0:n * P].rearrange("p (b k) -> p b k", k=P)).then_inc(pt_done, 1)

                def first_blocks():
                    row_max(0)
                    row_max(1)
                    normal(0)
                    normal(1)

                def head(b, h, slot, nxt, z):
                    if nxt:
                        take_qn(1 - b)
                    copy_turned(0)
                    row_max(2)
                    if nxt:
                        take_qr(1 - b)
                    normal(2)
                    copy_turned(1)
                    row_max(3)
                    copy_turned(2)
                    normal(3)
                    if nxt:
                        take_kn(1 - b)
                        take_vt(1 - b)
                    if z is not None:
                        unit.up(2)
                        dve.wait_ge(slot_free, unit.now() + RING)
                        zt.up()
                        dve.tensor_tensor(zs[:, z, :], aux[:, 0, :], rstd[:, :], ALU.mult).then_inc(z_taken, 1)
                        if not nxt:
                            silus.up()
                    copy_turned(3)
                    if nxt:
                        first_blocks()
                    dve.wait_ge(silu_done, silus.now())
                    dve.wait_ge(heads_done, hd.up())
                    dve.tensor_tensor(og[:, h, :], aux[:, 0, :], zs[:, slot, :], ALU.mult).then_inc(og_done, 1)
                    dve.wait_ge(og_done, hd.now())
                    if z is not None and nxt:
                        silus.up()

                sc, bs, en, tn, hd, zt = (Count() for _ in range(6))
                silus.up(8)
                dve.memset(small[:, 0:1], 0.0).then_inc(exp_done, 2)
                dve.wait_ge(exp_done, 2)
                dve.memset(small[:, 0:1], 0.0).then_inc(pt_done, 1)
                dve.wait_ge(pt_done, 1)
                take_qn(0)
                take_qr(0)
                take_kn(0)
                take_vt(0)
                first_blocks()
                for first, pairs in ((0, 4), (4, 3)):
                    with Rolled(dve, pairs, {unit: 8, tile: 8, sc: 8, bs: 8, en: 8, tn: 8, hd: 2, zt: 1, silus: 1,
                                             step: 24}) as i:
                        head(0, i * 2 + 2 * first, i * 2, True, None)
                        head(1, i * 2 + (2 * first + 1), i * 2 + 1, True, i + first)
                head(0, IT - 2, 6, True, None)
                head(1, IT - 1, 7, False, 7)
                for k in range(IT):
                    als.up()
                    dve.wait_ge(ah_done, als.now())
                    dve.tensor_tensor(act_l[:, k, :], og[:, k, :], act_h[:, k, :].bitcast(F32),
                                      ALU.subtract).then_inc(al_done, 1)

            def hybrid_mixer():
                link(dve.memset(cpad[:, 0:3], 0.0))
                link(dve.memset(rows[:, :], 0.0))
                link(dve.memset(reset[:, :], 1.0))
                link(dve.memset(reset[:, 0::CHUNK], 0.0))

                def conv_tile(n, f):
                    take(dve.tensor_tensor(cpad[:, 3:3 + S], bank(2), rstd[:, :], ALU.mult))
                    if n >= 2:
                        dve.wait_ge(heads_in, 2 * n - 3 if n - 2 < 8 else 16 + n - 9)
                    y_ = cy[:, n % 2, :]
                    link(dve.tensor_scalar(y_, cpad[:, 0:S], par("dn_conv", f), None, ALU.mult))
                    for k in (1, 2, 3):
                        ins = dve.scalar_tensor_tensor(y_, cpad[:, k:k + S], par("dn_conv", f + 12 * k), y_, ALU.mult, ALU.add)
                        if k < 3:
                            link(ins)
                    ins.then_inc(conv_done, 1)
                    dve.wait_ge(conv_done, n + 1)

                for i in range(8):
                    conv_tile(i, (i + 4) % 8)
                take(dve.tensor_tensor(raw[:, :], bank(2), rstd[:, :], ALU.mult))
                for i in range(4):
                    conv_tile(8 + i, 8 + i)

                def made(ins, name):
                    ins.then_inc(mix_dve, 1)
                    dve.wait_ge(mix_dve, DVE_STEP.next(name))

                rest_tiles = iter([(zc, h, 1.0) for h in HEADS]
                                  + [(a_q, 0, 0.125), (a_q, 1, 0.125), (a_kv, 0, 1.0), (a_kv, 1, 1.0), (b_q, 0, 0.125),
                                     (b_q, 1, 0.125), (b_k, 0, 1.0), (b_k, 1, 1.0), (b_v, 0, 1.0), (b_v, 1, 1.0)])

                def take_tile():
                    to, i, scale = next(rest_tiles)
                    take(dve.scalar_tensor_tensor(to[:, i, :], bank(2), scale, rstd[:, :], ALU.mult, ALU.mult))

                def normed(to, h, lengths, name, step):
                    dve.wait_ge(mix_act, ACT_STEP[step, h])
                    link(dve.reciprocal(lengths, lengths))
                    if name == "qf":
                        made(dve.scalar_tensor_tensor(to[:, h, :], lengths, P ** -0.5, to[:, h, :], ALU.mult, ALU.mult), (name, h))
                    else:
                        made(dve.tensor_tensor(to[:, h, :], to[:, h, :], lengths, ALU.mult), (name, h))

                def norm_key(h):
                    normed(kf, h, squares8[:, h, :], "kf", "sk")

                def norm_query(h):
                    normed(qf, h, squares8[:, 4 + h, :], "qf", "sq")

                dve.wait_ge(heads_in, 20)
                link(dve.tensor_scalar(raw[32:36, :], raw[32:36, :],
                                       params[32:36, PARAMS["dt_bias"]:PARAMS["dt_bias"] + 1], None, ALU.add))
                made(dve.scalar_tensor_tensor(absy[32:36, :], raw[32:36, :], -1.0, raw[32:36, :], ALU.mult, ALU.max), "ydt")
                take_tile()
                take_tile()
                norm_key(0)
                take_tile()
                norm_key(1)
                dve.wait_ge(mix_act, ACT_STEP["nega"])
                made(dve.tensor_scalar(rows[0:4, :], raw[0:4, :], 0.5, 0.5, ALU.mult, ALU.add), "beta")
                link(dve.scalar_tensor_tensor(raw[32:36, :], raw[32:36, :], 0.0, absy[32:36, :], ALU.max, ALU.add))
                link(dve.tensor_scalar(raw[32:36, :], raw[32:36, :], nega[32:36, :], -1.0, ALU.mult, ALU.mult))
                link(dve.tensor_tensor_scan(rows[32:36, :], reset[32:36, :], raw[32:36, :], 0.0, ALU.mult, ALU.add))
                made(dve.tensor_copy(rows[64:68, :].rearrange("p (c k) -> p c k", k=CHUNK),
                                     rows[32:36, CHUNK - 1::CHUNK].unsqueeze(2).broadcast_to([4, CHUNKS, CHUNK])), "g")
                take_tile()
                norm_key(2)
                take_tile()
                norm_key(3)
                dve.wait_ge(mix_pe, PE_STEP["rowt"])
                made(dve.tensor_copy(cols[:, :, :], head_bank(0, 0)[:, 0:4 * 68].rearrange("p (b k) -> p b k", k=68)), "cols")
                take_tile()
                norm_query(0)
                take_tile()
                dve.wait_ge(mix_act, ACT_STEP["cexp"])
                link(dve.tensor_tensor(cbe[:, :, :], cols[:, :, 0:4], ceg[:, :, :], ALU.mult))
                made(dve.tensor_tensor(ckd[:, :, :], cols[:, :, 64:68], cols[:, :, 32:36], ALU.subtract), "cd")
                for h in HEADS:
                    dve.wait_ge(mix_pe, PE_STEP["bb", h])
                    made(dve.tensor_tensor(kb[:, h, :], kf[:, h, :], head_bank(h, 0), ALU.mult), ("kb", h))
                take_tile()
                norm_query(1)
                dve.wait_ge(consts2_loaded, 16)
                mask_t = consts2[:, CONSTS2["mask_t"]:CONSTS2["mask_t"] + P]
                for h in HEADS:
                    dve.wait_ge(mix_pe, PE_STEP["bg", h])
                    for blk in range(4):
                        ins = dve.scalar_tensor_tensor(decay_of(h)[:, blk, :], head_bank(h, 0)[:, blk * P:blk * P + P],
                                                       cols[:, blk, 32 + h:33 + h], mask_t, ALU.subtract, ALU.add)
                    made(ins, ("dt", h))
                take_tile()
                norm_query(2)
                take_tile()
                norm_query(3)
                for h in HEADS:
                    dve.wait_ge(mix_pe, PE_STEP["kt", h])
                    for blk in range(4):
                        ins = dve.tensor_scalar(vf[:, h, blk * P:blk * P + P], head_bank(h, 0)[:, blk * P:blk * P + P],
                                                cbe[:, blk, h:h + 1], None, ALU.mult)
                    made(ins, ("kbe", h))
                take_tile()
                for h in HEADS:
                    dve.wait_ge(mix_pe, PE_STEP["g1", h])
                    made(dve.tensor_tensor(l_mat[:, h, :, :], blocks_of(head_bank(h, 0)), decay_of(h), ALU.mult), ("lt", h))
                    link(dve.tensor_tensor(xt[:, h, :, :], l_mat[:, h, :, :], level(0), ALU.mult))
                    made(dve.scalar_tensor_tensor(xt[:, h, :, :], xt[:, h, :, :], -1.0,
                                                  con("ident", P).unsqueeze(1).broadcast_to([P, 4, P]),
                                                  ALU.mult, ALU.add), ("xt0", h))
                take_tile()
                for h in HEADS:
                    dve.wait_ge(mix_pe, PE_STEP["g2", h])
                    made(dve.tensor_tensor(blocks_of(kf[:, h, :]), blocks_of(head_bank(h, 0)), decay_of(h),
                                           ALU.mult), ("at", h))
                take_tile()
                take_tile()
                for h in HEADS:
                    made(dve.tensor_tensor(e_mat[:, h, :, :], l_mat[:, h, :, :], level(1), ALU.mult), ("e1", h))
                for h in HEADS:
                    dve.wait_ge(mix_act, ACT_STEP["eg", h])
                    made(dve.tensor_tensor(blocks_of(qf[:, h, :]), blocks_of(qf[:, h, :]), eg[:, h, :, :], ALU.mult), ("qd", h))
                for l in range(1, LEVELS):
                    if l < LEVELS - 1:
                        for h in HEADS:
                            dve.wait_ge(mix_pe, PE_STEP[f"y{l}", h])
                            made(dve.tensor_tensor(e_mat[:, h, :, :], l_mat[:, h, :, :], level(l + 1), ALU.mult), (f"e{l + 1}", h))
                    for h in HEADS:
                        dve.wait_ge(mix_pe, PE_STEP[f"p{l}", h])
                        if l < LEVELS - 1:
                            link(dve.tensor_tensor(x_mat[:, h, :, :], x_mat[:, h, :, :], blocks_of(head_bank(h, 1)),
                                                   ALU.subtract))
                        made(dve.tensor_tensor(xt[:, h, :, :], xt[:, h, :, :], blocks_of(head_bank(h, 0)),
                                               ALU.subtract), (f"xt{l}", h))
                for i, slope in enumerate(SLOPES_SWA + SLOPES_MOBA):
                    ins = dve.tensor_scalar(slope_ident[:, i, :], con("ident", P), -slope, None, ALU.mult)
                made(ins, "slopes")

                def attend(k):
                    if 1 <= k <= PAIRS:
                        n = k - 1
                        tl, qb, first, w = pair_of(n)
                        sums = soft[:, n % 2, 1, :]
                        dve.wait_ge(mix_act, ACT_STEP["ex", n])
                        if tl < 2:
                            link(dve.tensor_tensor(sums, sums, soft[:, n % 2, 2, :], ALU.add))
                        link(dve.reciprocal(sums, sums))
                        for t in range(2):
                            ins = dve.tensor_scalar(probs[:, n % 2, t, 0:w], probs[:, n % 2, t, 0:w], sums[:, t:t + 1], None, ALU.mult)
                        made(ins, ("nr", n))
                    if k < PAIRS:
                        tl, qb, first, w = pair_of(k)
                        nmax, rest_of = soft[:, k % 2, 0, :], soft[:, k % 2, 2, :]
                        dve.wait_ge(mix_pe, PE_STEP["s", k])
                        link(dve.tensor_reduce(nmax, pair_scores(k), AX.X, ALU.max))
                        if tl < 2:
                            sinks = params[:, PARAMS["sinks"] + 2 * tl:PARAMS["sinks"] + 2 * tl + 2]
                            link(dve.tensor_tensor(nmax, nmax, sinks, ALU.max))
                            link(dve.tensor_scalar(nmax, nmax, -1.0, None, ALU.mult))
                            made(dve.tensor_tensor(rest_of, nmax, sinks, ALU.add), ("mx", k))
                        else:
                            made(dve.tensor_scalar(nmax, nmax, -1.0, None, ALU.mult), ("mx", k))

                for c in range(CHUNKS):
                    attend(2 * c)
                    if c < CHUNKS - 1:
                        dve.wait_ge(mix_pe, PE_STEP["su", c])
                        for h in HEADS:
                            if c:
                                ins = dve.scalar_tensor_tensor(state[:, h, :], state[:, h, :], egl[:, h, c:c + 1],
                                                               banks(0)[:, h * P:h * P + P], ALU.mult, ALU.add)
                            else:
                                ins = dve.tensor_copy(state[:, h, :], banks(0)[:, h * P:h * P + P])
                        made(ins, ("st", c))
                    attend(2 * c + 1)
                for k in (PAIRS, PAIRS + 1):
                    attend(k)
                dve.wait_ge(mix_act, ACT_STEP["osqrt"])
                made(dve.reciprocal(rc[:, :], rc[:, :]), "orc")

                def lo_of_mixed(k):
                    als.up()
                    dve.wait_ge(ah_done, als.now())
                    dve.tensor_tensor(act_l[:, k, :], mixed[:, k, :], act_h[:, k, :].bitcast(F32),
                                      ALU.subtract).then_inc(al_done, 1)

                for k in range(2):
                    lo_of_mixed(k)
                dve.wait_ge(mix_pe, PE_STEP["ornt"])
                made(dve.tensor_copy(rn[0:4, :], banks(0)[0:4, :]), "orn")
                for k in range(2, 4):
                    lo_of_mixed(k)
                for h in HEADS:
                    dve.wait_ge(mix_pe, PE_STEP["ob", h])
                    link(dve.scalar_tensor_tensor(mixed[:, 4 + h, :], mixed[:, 4 + h, :], par("dn_norm", 0), banks(4 + h),
                                                  ALU.mult, ALU.mult))
                    made(dve.tensor_tensor(mixed[:, 4 + h, :], mixed[:, 4 + h, :], zc[:, h, :], ALU.mult), ("on", h))
                    if h:
                        lo_of_mixed(3 + h)
                lo_of_mixed(7)

            dve.memset(ssum[:, :], 0.0).then_inc(taken, BANKS)
            dve.memset(std[:, :], 0.0).then_inc(slot_free, RING)
            dve.wait_ge(taken, BANKS)
            dve.wait_ge(slot_free, RING)
            dve.memset(rstd[:, :], 0.0).then_inc(ready, 1)
            dve.wait_ge(ready, 1)
            for f in range(DT):
                residual_tile(f, phases[0] != "final" and NORM_OF[phases[0]])
            deviation()
            for n, ph in enumerate(phases):
                nxt = NORM_OF[phases[n + 1]] if split_after(n) else None
                if ph in GROUPED:
                    dve.wait_ge(slot_free, unit.now() + RING + TOGETHER * 2)
                if ph.startswith("pool"):
                    link(dve.memset(upad[:, :, 0:PAD], 0.0))
                    for g, w in enumerate(WINDOWS):
                        for t in range(4):
                            u = upad[:, t % 2, :]
                            take(dve.tensor_tensor(u[:, PAD:PAD + S], bank(2), rstd[:, :], ALU.mult))
                            link(dve.tensor_tensor_scan(wsum[:, :], u[:, PAD:PAD + S], u[:, PAD - w:PAD - w + S],
                                                        0.0, ALU.add, ALU.subtract))
                            link(dve.tensor_tensor(wsum[:, 0:PAD], wsum[:, 0:PAD], con("poolfix", PAD, PAD * g),
                                                   ALU.mult))
                            dve.scalar_tensor_tensor(prod[:, :], wsum[:, :], 1.0 / w, u[:, PAD:PAD + S],
                                                     ALU.mult, ALU.subtract).then_inc(prod_done, 1)
                            dve.wait_ge(prod_done, prods.up())
                            rest(4 + 4 * g + t)
                    with Rolled(dve, 4, {unit: 12, tile: 8, silus: 4, als: 4}) as g:
                        for t in range(4):
                            take(dve.tensor_tensor(z4[:, t, :], bank(2), rstd[:, :], ALU.mult))
                        for t in range(4):
                            b = bank(1)
                            dve.wait_ge(silu_done, silus.up())
                            take(dve.scalar_tensor_tensor(prod[:, :], b, par("pool_scale" + ph[-1], g * 4 + t),
                                                          z4[:, t, :], ALU.mult, ALU.mult))
                            rest(g * 4 + t)
                    out_tiles(4, nxt)
                if ph == "conv":
                    link(dve.memset(qpad[:, 0:2], 0.0))
                    with Rolled(dve, IT, {unit: 8, tile: 4, silus: 1, als: 1, prods: 1, step: 5}) as f:
                        take(dve.tensor_tensor(cb[:, :], bank(2), rstd[:, :], ALU.mult))
                        take(dve.tensor_tensor(hb[:, :], bank(2), rstd[:, :], ALU.mult))
                        link(dve.tensor_tensor(qpad[:, 2:2 + S], cb[:, :], hb[:, :], ALU.mult))
                        link(dve.tensor_scalar(yb[:, :], qpad[:, 0:S], par("conv_w", f), None, ALU.mult))
                        for k in (1, 2):
                            link(dve.scalar_tensor_tensor(yb[:, :], qpad[:, k:k + S], par("conv_w", f + IT * k),
                                                          yb[:, :], ALU.mult, ALU.add))
                        take(dve.tensor_tensor(hb[:, :], bank(2), rstd[:, :], ALU.mult))
                        link(dve.tensor_tensor(yb[:, :], yb[:, :], hb[:, :], ALU.mult))
                        take(dve.tensor_tensor(zb[:, :], bank(2), rstd[:, :], ALU.mult))
                        dve.wait_ge(silu_done, silus.up())
                        dve.tensor_tensor(prod[:, :], yb[:, :], zb[:, :], ALU.mult).then_inc(prod_done, 1)
                        dve.wait_ge(prod_done, prods.up())
                        rest(f)
                    out_tiles(4, nxt)
                if ph == "mla":
                    latent_attention()
                    out_tiles(4, nxt)
                if ph == "final":
                    for f in range(DT):
                        dve.scalar_tensor_tensor(x[:, f, :], x[:, f, :], par("final_norm", f), rstd[:, :],
                                                 ALU.mult, ALU.mult).then_inc(x_done, 1)
                        dve.wait_ge(x_done, xs.up())
                        if f:
                            residual_tile(f - 1, nxt)
                    residual_tile(DT - 1, nxt)
                    deviation()
                if ph == "mixer":
                    hybrid_mixer()
                    out_tiles_of_y(2, "mix_post")
                    add_normed(nxt)
                if ph == "ffn":
                    link(dve.memset(gpad[:, :, 0:2], 0.0))

                    def conv3(t, f):
                        take(dve.tensor_tensor(gpad[:, t, 2:2 + S], bank(2), rstd[:, :], ALU.mult))
                        link(dve.tensor_scalar(yg[:, t, :], gpad[:, t, 0:S], par("ffn_conv_w", f),
                                               par("ffn_conv_b", f), ALU.mult, ALU.add))
                        link(dve.scalar_tensor_tensor(yg[:, t, :], gpad[:, t, 1:1 + S], par("ffn_conv_w", f + 2 * FT),
                                                      yg[:, t, :], ALU.mult, ALU.add))
                        return dve.scalar_tensor_tensor(yg[:, t, :], gpad[:, t, 2:2 + S],
                                                        par("ffn_conv_w", f + 4 * FT), yg[:, t, :], ALU.mult, ALU.add)

                    with Rolled(dve, FT // 2, {unit: 8, tile: 4, gates: 2, silus: 2, prods: 2, als: 2, step: 10}) as i:
                        for t in range(2):
                            f = i * 2 + t
                            conv3(0, f).then_inc(gate_done, 1)
                            gates.up()
                            if t:
                                rest(i * 2)
                            link(conv3(1, f + FT))
                            dve.wait_ge(silu_done, silus.up())
                            dve.tensor_tensor(prod[:, :], yg[:, 0, :], yg[:, 1, :], ALU.mult).then_inc(prod_done, 1)
                            dve.wait_ge(prod_done, prods.up())
                            if t:
                                rest(f)
                    out_tiles_of_y(6, "ffn_post")
                    add_normed(None)
            if phases[-1] != "ffn":
                dve.memset(ssum[:, :], 0.0).then_inc(x_done, 1)


NORM_OF = {"pool0": "pool_norm0", "pool1": "pool_norm1", "conv": "conv_norm", "mla": "mla_norm",
           "final": "final_norm", "mixer": "mix_pre", "ffn": "ffn_pre"}


def weight_blocks(a, phase):
    import numpy as np

    out = []

    def tile(w, cols, pad=None):
        ks = w.shape[0] // P
        for k in range(ks):
            out.append(w[k * P:(k + 1) * P, cols:cols + P])
        for _ in range((-ks) % 4 if pad is None else pad):
            out.append(np.zeros((P, P), np.float32))

    if phase.startswith("pool"):
        j = int(phase[-1])
        w_in, w_grp, w_out = a["pool_w_in"][j], a["pool_w_grp"][j], a["pool_w_out"][j]
        for f in range(IT):
            tile(w_in, f * P)
        for g in range(4):
            for t in range(4):
                tile(w_in, DI + (4 * g + t) * P)
            for t in range(4):
                tile(w_grp[g], t * P)
        for f in range(DT):
            tile(w_out, f * P)
    if phase == "conv":
        w_in = a["conv_w_in"][0]
        for f in range(IT):
            for part in (1, 2, 0, 3):
                tile(w_in, part * DI + f * P)
        for f in range(DT):
            tile(a["conv_w_out"][0], f * P)
    if phase == "mla":
        w_in, q_up, kv_up = a["mla_w_in"][0], a["mla_w_q_up"][0], a["mla_w_kv_up"][0]
        rope = w_in[:, 640:704]
        z_in = w_in[:, 704:]

        def with_halves_swapped(w):
            return np.concatenate([w, w[:, 32:], w[:, :32]], axis=1)

        def q_head(h):
            w = q_up[:, 192 * h:192 * h + 192]
            tile(w[:, :P], 0)
            tile(with_halves_swapped(w[:, P:]), 0)

        def kv_head(h):
            tile(kv_up, 256 * h, pad=0)
            tile(kv_up, 256 * h + P, pad=0)

        for f in range(5):
            tile(w_in, f * P)
        tile(with_halves_swapped(rope), 0)
        for f in range(8):
            tile(z_in, f * P)
        q_head(0)
        kv_head(0)
        for h in range(16):
            if h < 15:
                q_head(h + 1)
                kv_head(h + 1)
            if h % 2:
                tile(z_in, (8 + h // 2) * P)
        for f in range(DT):
            tile(a["mla_w_out"][0], f * P)
    if phase == "mixer":
        w = a["w_in_2"][0]
        q_a, k_a, v_a, q_b, k_b, v_b, qkv_c, z_c, b_c, a_c = np.split(
            w, np.cumsum([256, 128, 128, 256, 256, 256, 1536, 512, 4]), axis=1)
        for f in (4, 5, 6, 7, 0, 1, 2, 3):
            tile(qkv_c, f * P)
        ba = np.zeros((D, P), np.float32)
        ba[:, 0:4], ba[:, 32:36] = b_c, a_c
        tile(ba, 0)
        for f in range(8, 12):
            tile(qkv_c, f * P)
        for f in range(4):
            tile(z_c, f * P)
        tile(np.concatenate([q_a[:, 0:64], q_a[:, 128:192]], axis=1), 0)
        tile(np.concatenate([q_a[:, 64:128], q_a[:, 192:256]], axis=1), 0)
        tile(k_a, 0)
        tile(v_a, 0)
        for m in (q_b, k_b, v_b):
            tile(m, 0)
            tile(m, P)
        for f in range(DT):
            tile(a["w_out_2"][0], f * P)
    if phase == "ffn":
        for f in range(FT):
            tile(a["w_up_2"][0], f * P)
            tile(a["w_up_2"][0], FF + f * P)
        for f in range(DT):
            tile(a["w_down_2"][0], f * P)
    if phase in GROUPED:
        out[:TOGETHER * DT] = [out[i * DT + k] for k in range(DT) for i in range(TOGETHER)]
    return out


def pack(a, phases):
    import numpy as np

    blocks = [b for ph in phases for b in weight_blocks(a, ph)]
    blocks += [np.zeros((P, P), np.float32)] * (4 * n_units(phases) - len(blocks))
    w = np.stack(blocks).reshape(-1, 8, P, P)
    stream = np.ascontiguousarray(w.transpose(0, 2, 1, 3)).reshape(-1, P, 8 * P)

    params = np.zeros((P, NPARAMS), np.float32)

    def put(name, v, at=0):
        v = np.asarray(v).reshape(-1, P).T
        params[:, PARAMS[name] + at:PARAMS[name] + at + v.shape[1]] = v

    put("pool_norm0", a["pool_norm"][0]); put("pool_norm1", a["pool_norm"][1])
    put("conv_norm", a["conv_norm"][0]); put("mla_norm", a["mla_norm"][0]); put("final_norm", a["final_norm"])
    put("mix_pre", a["mix_pre_norm_2"][0]); put("mix_post", a["mix_post_norm_2"][0])
    put("ffn_pre", a["ffn_pre_norm_2"][0]); put("ffn_post", a["ffn_post_norm_2"][0])
    put("pool_scale0", a["pool_scale"][0]); put("pool_scale1", a["pool_scale"][1])
    put("conv_w", a["conv_w"][0]); put("q_norm", a["mla_q_norm"][0]); put("kv_norm", a["mla_kv_norm"][0])
    put("ffn_conv_w", a["ffn_conv_w_2"][0]); put("ffn_conv_b", a["ffn_conv_b_2"][0])
    put("dn_conv", a["dn_conv_w_2"][0]); put("dn_norm", a["dn_norm_2"][0])
    params[:, PARAMS["sinks"]:PARAMS["sinks"] + 4] = a["swa_sinks_2"][0][None, :]
    params[32:36, PARAMS["a_log"]] = a["dn_a_log_2"][0]
    params[32:36, PARAMS["dt_bias"]] = a["dn_dt_bias_2"][0]

    consts = np.zeros((P, NCONSTS), np.float32)
    p, c = np.arange(P)[:, None], np.arange(P)[None, :]
    consts[:, CONSTS["ident"]:CONSTS["ident"] + P] = p == c
    consts[:, CONSTS["fold"]:CONSTS["fold"] + P] = p % 64 == c % 64
    consts[:, CONSTS["causal"]:CONSTS["causal"] + P] = np.where(c <= p, 0.0, -1e30)
    for g, w in enumerate(WINDOWS):
        t = np.arange(PAD)
        consts[:, CONSTS["poolfix"] + g * PAD:CONSTS["poolfix"] + (g + 1) * PAD] = w / np.minimum(t + 1, w)
    i = np.arange(P)
    inv = 10000.0 ** (-2.0 * (i % 32) / 64)
    inv = inv.astype(np.float32)
    consts[:, CONSTS["freq"]] = np.where((i >= 64) & (i < 96), -inv, inv)
    consts[:, CONSTS["phase"]] = np.where(i < 64, np.float32(np.pi / 2), 0.0)
    consts[:, CONSTS["eps"]] = EPS
    c2 = np.zeros((P, NCONSTS2), np.float32)
    for l in range(LEVELS):
        s = 1 << l
        c2[:, l * P:l * P + P] = (p // (2 * s) == c // (2 * s)) & (p // s % 2 == 0) & (c // s % 2 == 1)
    c2[:, CONSTS2["mask_t"]:CONSTS2["mask_t"] + P] = np.where((p // CHUNK == c // CHUNK) & (c >= p), 0.0, -1e30)
    k = np.arange(4 * P)[None, :]
    c2[:, CONSTS2["dist"]:CONSTS2["dist"] + 4 * P] = np.where(p + 3 * P >= k, p + 3 * P - k, FAR)
    rel = p + P - k[:, :2 * P]
    c2[:, CONSTS2["dist_swa"]:CONSTS2["dist_swa"] + 2 * P] = np.where((rel >= 0) & (rel < P), rel, FAR)
    return {
        "consts2": c2,
        "x": np.ascontiguousarray(a["x"].reshape(S, DT, P).transpose(2, 1, 0)),
        "stream": stream, "params": params, "consts": consts,
        "pos": np.ascontiguousarray(np.broadcast_to(a["positions"].reshape(1, S), (P, S))),
    }


def kernel(**inputs):
    import numpy as np
    import concourse.bacc as bacc
    from concourse import mybir as mb
    from concourse.bass_utils import run_bass_kernel_spmd

    a = {k: np.asarray(v) for k, v in inputs.items()}
    arrays = pack(a, PHASES)
    nc = bacc.Bacc("TRN2", target_bir_lowering=False, num_devices=1)
    aps = {n: nc.dram_tensor(n, v.shape, mb.dt.from_np(v.dtype), kind="ExternalInput").ap() for n, v in arrays.items()}
    out = nc.dram_tensor("out", (P, DT, S), F32, kind="ExternalOutput").ap()
    program(nc, aps["x"], aps["stream"], aps["params"], aps["consts"], aps["consts2"], aps["pos"], out, PHASES)
    r = run_bass_kernel_spmd(nc, [arrays], core_ids=[0])
    return np.ascontiguousarray(r.results[0]["out"].transpose(2, 1, 0)).reshape(1, S, D)
```
